# Optimizing a Trainium2 kernel written in Bass

```python
import math
import jax, jax.numpy as jnp
from jax import lax
import numpy as np

D_MODEL = 1024
BATCH = 1
SEQ = 256
DEPTH = 1

MIX_WIDTH = D_MODEL
D_CONV = MIX_WIDTH // 2
D_SSM = MIX_WIDTH - D_CONV
CONV_HEAD_DIM = 64
CONV_HEADS = D_CONV // CONV_HEAD_DIM
CONV_WIDTH = 3
SSM_GROUP_CH = 16
SSM_GROUPS = D_SSM // SSM_GROUP_CH
SSM_STATE = 64
D_FF = 256 * ((8 * D_MODEL // 3 + 255) // 256)
N_MOD = 9
EPS = 1e-6
DT_MIN = 1e-3
DT_MAX = 1e-1


def rms_norm(x, gain):
    xf = x.astype(jnp.float32)
    y = xf * lax.rsqrt(jnp.mean(xf * xf, axis=-1, keepdims=True) + EPS)
    return (y * gain.astype(jnp.float32)).astype(x.dtype)

def modulate(h, shift, scale):
    return h * (1 + scale[:, None, :]) + shift[:, None, :]

def swiglu(h, w_gate, w_up, w_down):
    return (jax.nn.silu(h @ w_gate) * (h @ w_up)) @ w_down

def short_conv_mixer(b_gate, c_gate, v, conv_w):
    z = c_gate * v
    z = lax.conv_general_dilated(
        z, conv_w[:, None, :].astype(z.dtype),
        window_strides=(1,), padding=[(CONV_WIDTH - 1, 0)],
        dimension_numbers=('NWC', 'WIO', 'NWC'),
        feature_group_count=D_CONV)
    return b_gate * z

def _ssm_combine(left, right):
    a_l, b_l = left
    a_r, b_r = right
    return a_r * a_l, a_r * b_l + b_r

def s5_mixer(u, lambda_re, lambda_im, log_dt, b_re, b_im, c_re, c_im, d_skip, glu_w, glu_b):
    bsz, seq, _ = u.shape
    uf = u.astype(jnp.float32).reshape(bsz, seq, SSM_GROUPS, SSM_GROUP_CH)
    lam = lax.complex(lambda_re.astype(jnp.float32), lambda_im.astype(jnp.float32))
    dt = jnp.exp(log_dt.astype(jnp.float32))[:, None]
    lam_bar = jnp.exp(lam * dt)
    b = lax.complex(b_re.astype(jnp.float32), b_im.astype(jnp.float32))
    b_bar = ((lam_bar - 1) / lam)[..., None] * b
    bu = jnp.einsum('gpc,bsgc->bsgp', b_bar, uf.astype(jnp.complex64))
    a = jnp.broadcast_to(lam_bar, bu.shape)
    _, states = lax.associative_scan(_ssm_combine, (a, bu), axis=1)
    c = lax.complex(c_re.astype(jnp.float32), c_im.astype(jnp.float32))
    y = jnp.einsum('gcp,bsgp->bsgc', c, states).real \
        + d_skip.astype(jnp.float32).reshape(SSM_GROUPS, SSM_GROUP_CH) * uf
    y = jax.nn.gelu(y.reshape(bsz, seq, D_SSM))
    y = y * jax.nn.sigmoid(y @ glu_w.astype(jnp.float32) + glu_b.astype(jnp.float32))
    return y.astype(u.dtype)

def first_inputs(seed: int = 0) -> dict:
    key = jax.random.key(seed)
    ks = jax.random.split(key, 32)
    f32 = jnp.float32

    def nrm(k, shape, std):
        return jax.random.normal(k, shape, f32) * std

    def gain(k, shape):
        return 1.0 + 0.05 * jax.random.normal(k, shape, f32)

    L = DEPTH
    n_idx = jnp.arange(SSM_STATE, dtype=f32)
    return {
        "x": nrm(ks[0], (BATCH, SEQ, D_MODEL), 1.0),
        "cond": nrm(ks[1], (BATCH, D_MODEL), 1.0),
        "w_mod": nrm(ks[2], (L, D_MODEL, N_MOD * D_MODEL), 0.5 * D_MODEL ** -0.5),
        "b_mod": nrm(ks[3], (L, N_MOD * D_MODEL), 0.02),
        "ffn1_norm": gain(ks[4], (L, D_MODEL)),
        "ffn1_w_gate": nrm(ks[5], (L, D_MODEL, D_FF), D_MODEL ** -0.5),
        "ffn1_w_up": nrm(ks[6], (L, D_MODEL, D_FF), D_MODEL ** -0.5),
        "ffn1_w_down": nrm(ks[7], (L, D_FF, D_MODEL), D_FF ** -0.5),
        "mix_norm": gain(ks[8], (L, D_MODEL)),
        "w_in": nrm(ks[9], (L, D_MODEL, 3 * D_CONV + D_SSM), D_MODEL ** -0.5),
        "conv_w": nrm(ks[10], (L, CONV_WIDTH, D_CONV), CONV_WIDTH ** -0.5),
        "lambda_re": -0.5 + 0.01 * jax.random.normal(ks[11], (L, SSM_GROUPS, SSM_STATE), f32),
        "lambda_im": math.pi * n_idx + 0.01 * jax.random.normal(ks[12], (L, SSM_GROUPS, SSM_STATE), f32),
        "log_dt": jax.random.uniform(ks[13], (L, SSM_GROUPS), f32, math.log(DT_MIN), math.log(DT_MAX)),
        "ssm_b_re": nrm(ks[14], (L, SSM_GROUPS, SSM_STATE, SSM_GROUP_CH), (2 * SSM_GROUP_CH) ** -0.5),
        "ssm_b_im": nrm(ks[15], (L, SSM_GROUPS, SSM_STATE, SSM_GROUP_CH), (2 * SSM_GROUP_CH) ** -0.5),
        "ssm_c_re": nrm(ks[16], (L, SSM_GROUPS, SSM_GROUP_CH, SSM_STATE), SSM_STATE ** -0.5),
        "ssm_c_im": nrm(ks[17], (L, SSM_GROUPS, SSM_GROUP_CH, SSM_STATE), SSM_STATE ** -0.5),
        "ssm_d": nrm(ks[18], (L, D_SSM), 1.0),
        "glu_w": nrm(ks[19], (L, D_SSM, D_SSM), D_SSM ** -0.5),
        "glu_b": nrm(ks[20], (L, D_SSM), 0.02),
        "out_norm_conv": gain(ks[21], (L, D_CONV)),
        "out_norm_ssm": gain(ks[22], (L, D_SSM)),
        "w_out": nrm(ks[23], (L, MIX_WIDTH, D_MODEL), MIX_WIDTH ** -0.5),
        "ffn2_norm": gain(ks[24], (L, D_MODEL)),
        "ffn2_w_gate": nrm(ks[25], (L, D_MODEL, D_FF), D_MODEL ** -0.5),
        "ffn2_w_up": nrm(ks[26], (L, D_MODEL, D_FF), D_MODEL ** -0.5),
        "ffn2_w_down": nrm(ks[27], (L, D_FF, D_MODEL), D_FF ** -0.5),
        "final_norm": gain(ks[28], (D_MODEL,)),
    }

def first_block(x, cond, w_mod, b_mod, ffn1_norm, ffn1_w_gate, ffn1_w_up, ffn1_w_down,
              mix_norm, w_in, conv_w, lambda_re, lambda_im, log_dt,
              ssm_b_re, ssm_b_im, ssm_c_re, ssm_c_im, ssm_d, glu_w, glu_b,
              out_norm_conv, out_norm_ssm, w_out,
              ffn2_norm, ffn2_w_gate, ffn2_w_up, ffn2_w_down, final_norm):
    c_act = jax.nn.silu(cond)
    for l in range(DEPTH):
        mod = c_act @ w_mod[l] + b_mod[l]
        (sh1, sc1, g1, sh2, sc2, g2, sh3, sc3, g3) = jnp.split(mod, N_MOD, axis=-1)

        h = modulate(rms_norm(x, ffn1_norm[l]), sh1, sc1)
        x = x + 0.5 * g1[:, None, :] * swiglu(h, ffn1_w_gate[l], ffn1_w_up[l], ffn1_w_down[l])

        h = modulate(rms_norm(x, mix_norm[l]), sh2, sc2)
        proj = h @ w_in[l]
        b_gate, c_gate, v, u = jnp.split(proj, [D_CONV, 2 * D_CONV, 3 * D_CONV], axis=-1)
        y_conv = short_conv_mixer(b_gate, c_gate, v, conv_w[l])
        y_ssm = s5_mixer(u, lambda_re[l], lambda_im[l], log_dt[l], ssm_b_re[l], ssm_b_im[l],
                         ssm_c_re[l], ssm_c_im[l], ssm_d[l], glu_w[l], glu_b[l])
        y_mix = jnp.concatenate([rms_norm(y_conv, out_norm_conv[l]),
                                 rms_norm(y_ssm, out_norm_ssm[l])], axis=-1)
        x = x + g2[:, None, :] * (y_mix @ w_out[l])

        h = modulate(rms_norm(x, ffn2_norm[l]), sh3, sc3)
        x = x + 0.5 * g3[:, None, :] * swiglu(h, ffn2_w_gate[l], ffn2_w_up[l], ffn2_w_down[l])
    return rms_norm(x, final_norm)


DEPTH_2 = 2

N_A = DEPTH_2 // 2
N_B = DEPTH_2 - N_A

GLA_HEADS = 4
GLA_DK = (D_MODEL // 2) // GLA_HEADS
GLA_DV = D_MODEL // GLA_HEADS
GLA_GATE_RANK = 16
GLA_TAU = 16.0
GLA_CHUNK = 64
GLA_COLS = (GLA_HEADS * GLA_DK, GLA_HEADS * GLA_DK, GLA_HEADS * GLA_DV, GLA_HEADS * GLA_DV, GLA_GATE_RANK)
GLA_SPLITS = list(np.cumsum(GLA_COLS)[:-1].tolist())
GLA_IN = int(sum(GLA_COLS))

DIFF_HEADS = 8
DIFF_DH = 64
DIFF_VD = 2 * DIFF_DH
Q_BLOCK = 128

MLP_HIDDEN = 4 * D_MODEL
NORM_EPS = 1e-6


def rms_norm_2(x, g):
    xf = x.astype(jnp.float32)
    y = xf * lax.rsqrt(jnp.mean(xf * xf, axis=-1, keepdims=True) + NORM_EPS)
    return (y * g.astype(jnp.float32)).astype(x.dtype)

def sqrelu_mlp(xn, w1, w2):
    return jnp.square(jax.nn.relu(xn @ w1)) @ w2

def gla_chunked(q, k, v, log_a):
    B, S, H, DK = q.shape
    DV = v.shape[-1]
    C = GLA_CHUNK
    n = S // C

    def chunks(t):
        return t.astype(jnp.float32).reshape(B, n, C, H, t.shape[-1]).transpose(1, 0, 3, 2, 4)

    qc = chunks(q) * (DK ** -0.5)
    kc = chunks(k)
    vc = chunks(v)
    bc = jnp.cumsum(chunks(log_a), axis=-2)
    causal = jnp.tril(jnp.ones((C, C), bool))

    def step(state, inp):
        qi, ki, vi, bi = inp
        diff = bi[:, :, :, None, :] - bi[:, :, None, :, :]
        decay = jnp.exp(jnp.where(causal[:, :, None], diff, -jnp.inf))
        attn = jnp.einsum('bhid,bhjd,bhijd->bhij', qi, ki, decay)
        o = (jnp.einsum('bhij,bhjv->bhiv', attn, vi)
             + jnp.einsum('bhid,bhdv->bhiv', qi * jnp.exp(bi), state))
        b_last = bi[:, :, -1:, :]
        state = (jnp.exp(b_last[:, :, 0, :, None]) * state
                 + jnp.einsum('bhjd,bhjv->bhdv', ki * jnp.exp(b_last - bi), vi))
        return state, o

    _, o = lax.scan(step, jnp.zeros((B, H, DK, DV), jnp.float32), (qc, kc, vc, bc))
    return o.transpose(1, 0, 3, 2, 4).reshape(B, S, H, DV)

def gla_mixer(xn, w_in, w_gate_up, b_gate, head_gain, w_out):
    B, S, _ = xn.shape
    proj = xn @ w_in
    q, k, v, g, z = jnp.split(proj, GLA_SPLITS, axis=-1)
    log_a = jax.nn.log_sigmoid((z @ w_gate_up + b_gate).astype(jnp.float32)) / GLA_TAU
    hk = lambda t: t.reshape(B, S, GLA_HEADS, GLA_DK)
    o = gla_chunked(hk(q), hk(k), v.reshape(B, S, GLA_HEADS, GLA_DV), hk(log_a)).astype(xn.dtype)
    o = rms_norm_2(o, head_gain) * jax.nn.silu(g.reshape(B, S, GLA_HEADS, GLA_DV))
    return o.reshape(B, S, GLA_HEADS * GLA_DV) @ w_out

def shared_kv(h, kv_norm, w_kv, k_norm):
    B, S, _ = h.shape
    kv = rms_norm_2(h, kv_norm) @ w_kv
    k, v = jnp.split(kv, [DIFF_HEADS * 2 * DIFF_DH], axis=-1)
    k = rms_norm_2(k.reshape(B, S, DIFF_HEADS, 2, DIFF_DH), k_norm).transpose(0, 2, 3, 1, 4)
    v = v.reshape(B, S, DIFF_HEADS, DIFF_VD).transpose(0, 2, 1, 3)
    return k, v

def diff_mixer(xn, k, v, w_q, q_gain, lam_params, head_gain, w_out, lambda_init):
    B, S, _ = xn.shape
    q = rms_norm_2((xn @ w_q).reshape(B, S, DIFF_HEADS, 2, DIFF_DH), q_gain) * (DIFF_DH ** -0.5)
    lp = lam_params.astype(jnp.float32)
    lam = jnp.exp(jnp.sum(lp[0] * lp[1])) - jnp.exp(jnp.sum(lp[2] * lp[3])) + lambda_init
    nq = S // Q_BLOCK
    qb = q.transpose(0, 2, 3, 1, 4).reshape(B, DIFF_HEADS, 2, nq, Q_BLOCK, DIFF_DH).transpose(3, 0, 1, 2, 4, 5)
    kpos = jnp.arange(S)

    def attend(args):
        q_blk, bi = args
        s = jnp.einsum('bhcqd,bhckd->bhcqk', q_blk, k).astype(jnp.float32)
        qpos = bi * Q_BLOCK + jnp.arange(Q_BLOCK)
        s = jnp.where(kpos[None, :] <= qpos[:, None], s, -jnp.inf)
        p = jax.nn.softmax(s, axis=-1)
        a = p[:, :, 0] - lam * p[:, :, 1]
        return jnp.einsum('bhqk,bhkv->bhqv', a.astype(v.dtype), v)

    o = lax.map(attend, (qb, jnp.arange(nq)))
    o = o.transpose(1, 0, 3, 2, 4).reshape(B, S, DIFF_HEADS, DIFF_VD)
    o = rms_norm_2(o, head_gain) * (1.0 - lambda_init)
    return o.reshape(B, S, DIFF_HEADS * DIFF_VD) @ w_out

def second_inputs(seed: int = 0) -> dict:
    key = jax.random.key(seed)
    ks = jax.random.split(key, 24)
    f32 = jnp.float32
    nrm = lambda k, shape, fan_in: jax.random.normal(k, shape, f32) * (fan_in ** -0.5)
    gain = lambda k, shape: 1.0 + 0.02 * jax.random.normal(k, shape, f32)
    D = D_MODEL
    return {
        "x": jax.random.normal(ks[0], (BATCH, SEQ, D), f32),
        "a_norm": gain(ks[1], (N_A, D)),
        "a_w_in": nrm(ks[2], (N_A, D, GLA_IN), D),
        "a_w_gate_up": nrm(ks[3], (N_A, GLA_GATE_RANK, GLA_HEADS * GLA_DK), GLA_GATE_RANK),
        "a_b_gate": 0.1 * jax.random.normal(ks[4], (N_A, GLA_HEADS * GLA_DK), f32),
        "a_head_norm": gain(ks[5], (N_A, GLA_DV)),
        "a_w_out": nrm(ks[6], (N_A, GLA_HEADS * GLA_DV, D), GLA_HEADS * GLA_DV),
        "kv_norm": gain(ks[7], (D,)),
        "w_kv": nrm(ks[8], (D, DIFF_HEADS * (2 * DIFF_DH + DIFF_VD)), D),
        "k_norm": gain(ks[9], (DIFF_DH,)),
        "b_norm": gain(ks[10], (N_B, D)),
        "b_w_q": nrm(ks[11], (N_B, D, DIFF_HEADS * 2 * DIFF_DH), D),
        "b_q_norm": gain(ks[12], (N_B, DIFF_DH)),
        "b_lambda": 0.1 * jax.random.normal(ks[13], (N_B, 4, DIFF_DH), f32),
        "b_head_norm": gain(ks[14], (N_B, DIFF_VD)),
        "b_w_out": nrm(ks[15], (N_B, DIFF_HEADS * DIFF_VD, D), DIFF_HEADS * DIFF_VD),
        "mlp_norm": gain(ks[16], (DEPTH_2, D)),
        "mlp_w1": nrm(ks[17], (DEPTH_2, D, MLP_HIDDEN), D),
        "mlp_w2": nrm(ks[18], (DEPTH_2, MLP_HIDDEN, D), MLP_HIDDEN),
    }

def second_block(x, a_norm, a_w_in, a_w_gate_up, a_b_gate, a_head_norm, a_w_out,
              kv_norm, w_kv, k_norm, b_norm, b_w_q, b_q_norm, b_lambda, b_head_norm, b_w_out,
              mlp_norm, mlp_w1, mlp_w2):
    h = x
    k_sh, v_sh = None, None
    for layer in range(DEPTH_2):
        if layer < N_A:
            i = layer
            h = h + gla_mixer(rms_norm_2(h, a_norm[i]), a_w_in[i], a_w_gate_up[i], a_b_gate[i],
                              a_head_norm[i], a_w_out[i])
        else:
            if layer == N_A:
                k_sh, v_sh = shared_kv(h, kv_norm, w_kv, k_norm)
            j = layer - N_A
            lambda_init = 0.8 - 0.6 * math.exp(-0.3 * layer)
            h = h + diff_mixer(rms_norm_2(h, b_norm[j]), k_sh, v_sh, b_w_q[j], b_q_norm[j],
                               b_lambda[j], b_head_norm[j], b_w_out[j], lambda_init)
        h = h + sqrelu_mlp(rms_norm_2(h, mlp_norm[layer]), mlp_w1[layer], mlp_w2[layer])
    return h


def setup_inputs(seed=0):
    out = dict(first_inputs(seed))
    for name, value in second_inputs(seed + 1).items():
        if name != "x":
            out[name + "_2"] = value
    return out


def reference(
    x, cond, w_mod, b_mod, ffn1_norm, ffn1_w_gate, ffn1_w_up, ffn1_w_down, mix_norm, w_in,
    conv_w, lambda_re, lambda_im, log_dt, ssm_b_re, ssm_b_im, ssm_c_re, ssm_c_im, ssm_d, glu_w,
    glu_b, out_norm_conv, out_norm_ssm, w_out, ffn2_norm, ffn2_w_gate, ffn2_w_up, ffn2_w_down,
    final_norm, a_norm_2, a_w_in_2, a_w_gate_up_2, a_b_gate_2, a_head_norm_2, a_w_out_2,
    kv_norm_2, w_kv_2, k_norm_2, b_norm_2, b_w_q_2, b_q_norm_2, b_lambda_2, b_head_norm_2,
    b_w_out_2, mlp_norm_2, mlp_w1_2, mlp_w2_2,
):
    x = first_block(
        x, cond, w_mod, b_mod, ffn1_norm, ffn1_w_gate, ffn1_w_up, ffn1_w_down, mix_norm, w_in,
        conv_w, lambda_re, lambda_im, log_dt, ssm_b_re, ssm_b_im, ssm_c_re, ssm_c_im, ssm_d,
        glu_w, glu_b, out_norm_conv, out_norm_ssm, w_out, ffn2_norm, ffn2_w_gate, ffn2_w_up,
        ffn2_w_down, final_norm,
    )
    return second_block(
        x, a_norm_2, a_w_in_2, a_w_gate_up_2, a_b_gate_2, a_head_norm_2, a_w_out_2, kv_norm_2,
        w_kv_2, k_norm_2, b_norm_2, b_w_q_2, b_q_norm_2, b_lambda_2, b_head_norm_2, b_w_out_2,
        mlp_norm_2, mlp_w1_2, mlp_w2_2,
    )


_drawn_inputs = setup_inputs


def setup_inputs(seed=0):
    import zlib

    import numpy as np

    out = dict(_drawn_inputs(seed))
    spreads = {}
    factors = {'ffn1_norm': 4.941,
     'lambda_re': 8.0,
     'glu_b': 8.0,
     'out_norm_conv': 3.511,
     'out_norm_ssm': 3.111,
     'ffn2_norm': 5.462,
     'a_head_norm_2': 5.004,
     'kv_norm_2': 6.974,
     'k_norm_2': 8.0,
     'b_norm_2': 8.0,
     'b_q_norm_2': 8.0,
     'b_head_norm_2': 7.768}
    for name, (base, spread) in spreads.items():
        noise = np.random.default_rng([zlib.crc32(name.encode()), seed]).standard_normal(out[name].shape)
        drawn = base * np.exp(spread * noise) if base else spread * noise
        out[name] = __import__('jax').numpy.asarray(drawn.astype(out[name].dtype))
    for name, factor in factors.items():
        out[name] = (out[name] * factor).astype(out[name].dtype)
    return out
```

```python
import math
from contextlib import ExitStack

import concourse.bass as bass
from concourse import mybir

F32 = mybir.dt.float32
F32R = mybir.dt.float32r
ACT = mybir.ActivationFunctionType
ALU = mybir.AluOpType
AX = mybir.AxisListType

P = 128
S = 256
D = 1024
KD = D // P
FF = 2816
NF = FF // P
HID = 4096
NHID = HID // P
EPS = 1e-6
N_MOD = 9
MODC = 256
NMODC = N_MOD * D // MODC
MOD0 = 2 * D // MODC
MOD_TAIL = {NF - 3: [28, 29, 30], NF - 2: [31, 32, 33], NF - 1: [34, 35]}
GRP, GCH, NST = 32, 16, 64
ST = GRP * NST // P
GH, GDK, GDV = 4, 128, 256
GBLK = 32
NBLK = S // GBLK
KTOT = sum(GBLK * (b + 1) for b in range(NBLK))
TAU = 16.0
DH = 8
DD = 64
LAM_INIT = 0.8 - 0.6 * math.exp(-0.3)
MASKED = -1e30
ROUND = 1.5 * 2 ** 23

A_STAGES = [
    ("ffn1", NF, 2048, 1), ("w_in", 8, 2048, 1), ("glu", 2, 1024, 1), ("w_out", 4, 2048, 1),
    ("ffn2", NF, 2048, 1),
    ("a_qk", 4, 2048, 1), ("a_v", 4, 2048, 0), ("a_g", 4, 2048, 1), ("a_out", 4, 2048, 1),
    ("mlp0", NHID, 1024, 1),
    ("b_k", 4, 2048, 1), ("b_v", 4, 2048, 0), ("b_q", 4, 2048, 1), ("b_out", 4, 2048, 1),
    ("mlp1", NHID, 1024, 1),
]
NEXT = {a[0]: b[0] for a, b in zip(A_STAGES, A_STAGES[1:])}
A_BASE, GU_BASE, A_LEN, A_SIZE = {}, {}, {}, {}
_a = _g = 0
for _name, _n, _size, _gu in A_STAGES:
    A_BASE[_name], GU_BASE[_name], A_LEN[_name], A_SIZE[_name] = _a, _g, _n, _size
    _a += _n
    _g += _n * _gu
D_STAGES = [("ffn1", NF), ("ffn2", NF), ("mlp0", NHID), ("mlp1", NHID)]
D_BASE, _d = {}, 0
for _name, _n in D_STAGES:
    D_BASE[_name] = _d
    _d += _n
D_TOTAL = _d
A_ORDER = [(s, c) for s, n, _, _ in A_STAGES for c in range(n)]
WIN_TILES = [12, 13, 14, 15, 4, 5, 8, 9, 6, 7, 10, 11, 0, 1, 2, 3]
NORMS = ["ffn1", "mix", "ffn2", "final", "a", "mlp0", "kv", "b", "mlp1"]

V0 = {"b_mod": (0, 72), "cond": (72, 8)}
V1_ROWS = [("ffn1_norm", 8), ("mix_norm", 8), ("ffn2_norm", 8), ("final_norm", 8), ("a_norm_2", 8),
           ("kv_norm_2", 8), ("b_norm_2", 8), ("mlp_norm_2", 16), ("out_norm_conv", 4),
           ("out_norm_ssm", 4), ("ssm_d", 4), ("glu_b", 4), ("a_b_gate_2", 4), ("conv_w", 12),
           ("a_head_norm_2", 2), ("b_head_norm_2", 1)]
V2_ROWS = [("lambda_re", 16), ("lambda_im", 16), ("k_norm_2", 1), ("b_q_norm_2", 1)]


def columns(rows):
    at, out = 0, {}
    for name, n in rows:
        out[name] = (at, n)
        at += n
    return out, at


V1, V1_N = columns(V1_ROWS)
V2, V2_N = columns(V2_ROWS)


ORDER = ["ffn1", "mix", "glu", "conv", "ssm", "ymix", "ffn2", "final", "a", "oa", "mlp0", "kv", "b", "ob", "mlp1"]
COUNTS = {
    "sq": {"conv": 1, "ssm": 1, "glu": 0, "ymix": 0, "oa": 0, "b": 0, "ob": 0},
    "ss": {"glu": 0, "ymix": 0, "oa": 0, "b": 0, "ob": 0},
    "root": {"glu": 0, "ymix": 0, "oa": 0, "b": 0, "ob": 0},
    "rstd": {"glu": 0, "conv": 0, "ssm": 0, "ymix": 0, "oa": 0, "b": 0, "ob": 0},
    "t": {"glu": 0, "conv": 0, "ssm": 0, "final": 0},
    "hh": {"glu": 4, "conv": 0, "ssm": 0, "final": 0},
    "h": {"glu": 4, "conv": 0, "ssm": 0, "final": 0},
}
EACH = {"sq": 2, "ss": 1, "root": 1, "rstd": 1, "t": KD, "hh": KD, "h": KD}


def after(kind, name, v):
    return v + sum(COUNTS[kind].get(n, EACH[kind]) for n in ORDER[:ORDER.index(name)])


def lin(v, i, m):
    return v if i is None else i * m + v


def build(nc, T, out):
    ctx = ExitStack()
    with ctx:
        def sb(name, shape, dt=F32):
            return ctx.enter_context(nc.sbuf_tensor(name, shape, dt))

        sems = {}

        def sem(name):
            if name not in sems:
                sems[name] = ctx.enter_context(nc.semaphore(name))
            return sems[name]

        x_t = sb("x_t", [P, KD, S])
        h_hi = sb("h_hi", [P, KD, S], F32R)
        h_lo = sb("h_lo", [P, KD, S], F32R)
        tmp = sb("tmp", [P, KD, S])
        raw_a = sb("raw_a", [P, 2, 2048])
        hi_a = sb("hi_a", [P, 2, 2048], F32R)
        lo_a = sb("lo_a", [P, 2, 2048], F32R)
        raw_d = sb("raw_d", [P, 2, D])
        hi_d = sb("hi_d", [P, 2, D], F32R)
        lo_d = sb("lo_d", [P, 2, D], F32R)
        raw_m = sb("raw_m", [P, 2, KD, MODC])
        acc_m = sb("acc_m", [P, 2, MODC])
        gate = sb("gate", [P, 2, S])
        hid = sb("hid", [P, 2, S])
        hid_hi = sb("hid_hi", [P, 2, S], F32R)
        hid_lo = sb("hid_lo", [P, 2, S], F32R)
        root, rstd = hid, gate
        ident = sb("ident", [P, P])
        ones = sb("ones", [P, P])
        ones_blk = sb("ones_blk", [P, P])
        eps = sb("eps", [P, 1])
        v0_rows, v1_rows, v2_rows = gate[0:80, 0, 0:P], gate[0:V1_N, 0, P:S], gate[0:V2_N, 1, 0:P]
        v0 = sb("v0", [P, 80])
        v1 = sb("v1", [P, V1_N])
        v2 = sb("v2", [P, V2_N])
        cact = sb("cact", [P, KD])
        mod = sb("mod", [P, N_MOD * KD])
        nscale = sb("nscale", [P, 3, KD])
        ghalf = sb("ghalf", [P, 2, KD])
        arena = sb("arena", [P, 13312])
        ps = ctx.enter_context(nc.psum_tensor("ps", [P, 8, 512], F32))
        psf = ps[:, :, :].rearrange("p b n -> p (b n)")
        acc4 = psf[:, 1024:3072]

        def area(at, n):
            return arena[:, at:at + n]

        def tiles(ap, n=S):
            return ap.rearrange("p (t n) -> p t n", n=n)

        raw_m_flat = raw_m[:, :, :, :].rearrange("p a k n -> p (a k n)")
        tmp_flat = tmp[:, :, :].rearrange("p k n -> p (k n)")

        proj = tiles(area(0, 4096))
        ph_re, ph_im = tiles(area(4096, 4096)), tiles(area(8192, 4096))
        y_ssm = tiles(area(12288, 1024))
        w_re, w_im = tmp_flat[:, 0:1024], tmp_flat[:, 1024:2048]
        prod = [raw_m_flat[:, 1024 * k:1024 * (k + 1)] for k in range(4)]
        conv_sum = sb("conv_sum", [P, 4, S])
        dt_col = sb("dt_col", [P, ST])
        s5 = sb("s5", [P, 19, ST])
        b_bd = conv_sum[:, :, :].rearrange("p t n -> p (t n)").rearrange("p (r t c) -> p r t c", r=2, c=2 * GCH)
        b_t = sb("b_t", [P, 2, 4, P])
        c_in = area(12288, 1024).rearrange("p (r u n) -> p r u n", r=2, u=4)
        c_t = sb("c_t", [P, 3, 4, P])
        b_in = c_t[:, 0].rearrange("p u n -> p (u n)").rearrange("p (r t c) -> p r t c", r=2, c=GCH)
        zw = sb("zw", [P, KD, 16])
        gup = sb("gup", [16, GH * GDK])
        z_sb = sb("z_sb", [16, S])
        tri = sb("tri", [P, P])
        bias_mask = sb("bias_mask", [P, 384])
        lamp = sb("lamp", [P, 4, DD])
        lam_s = sb("lam_s", [P, 8])

        qk = tiles(area(0, 2048))
        v_rows = area(2048, 2048).rearrange("p (t n) -> p t n", t=2)
        silu_g = tiles(area(4096, 2048))
        cum = area(6144, 1024)
        q_dec = area(7168, 1024)
        k_dec = area(8192, GH * KTOT)
        at_sb = tmp_flat
        k_n = tiles(area(0, 2048))
        q_n = tiles(area(4096, 2048))
        zero_w = sb("zero_w", [P, P], F32R)
        s_sb = area(6144, 2 * 768)
        p_sb = area(7680, 2 * 768)
        a_sb = area(9216, 2 * 384)
        a_t = area(9984, 2 * 384)
        st_lam = sb("st_lam", [P, 2, DD])
        qgain = sb("qgain", [P, 1])
        st_s = sb("st_s", [P, 2, 16])

        gate_flat = gate[:, :, :].rearrange("p t n -> p (t n)")

        def vec(tile, table, name, k, n=1):
            at = table[name][0]
            return tile[:, at + k:at + k + n]

        def bcast(ap, n):
            return ap.unsqueeze(2).to_broadcast([ap.shape[0], ap.shape[1], n])

        def kt(w, k=KD):
            return w.rearrange("(k p) n -> p k n", p=P)

        wv = {
            "g1": kt(T["ffn1_w_gate"][0]), "u1": kt(T["ffn1_w_up"][0]),
            "g2": kt(T["ffn2_w_gate"][0]), "u2": kt(T["ffn2_w_up"][0]),
            "w_in": kt(T["w_in"][0]), "glu": kt(T["glu_w"][0]), "w_out": kt(T["w_out"][0]),
            "a_in": kt(T["a_w_in_2"][0]), "a_out": kt(T["a_w_out_2"][0]),
            "kv": kt(T["w_kv_2"]), "b_q": kt(T["b_w_q_2"][0]), "b_out": kt(T["b_w_out_2"][0]),
            "mlp0": kt(T["mlp_w1_2"][0]), "mlp1": kt(T["mlp_w1_2"][1]),
            "mod": kt(T["w_mod"][0]),
        }
        dv = {"ffn1": kt(T["ffn1_w_down"][0]), "ffn2": kt(T["ffn2_w_down"][0]),
              "mlp0": kt(T["mlp_w2_2"][0]), "mlp1": kt(T["mlp_w2_2"][1])}

        a_loaded = [sem("a_loaded0"), sem("a_loaded1")]
        d_loaded = [sem("d_loaded0"), sem("d_loaded1")]
        m_loaded = [sem("m_loaded0"), sem("m_loaded1")]
        a_hi, a_split, a_used = sem("a_hi"), sem("a_split"), sem("a_used")
        d_hi, d_split, d_used = sem("d_hi"), sem("d_split"), sem("d_used")
        m_summed, m_step = sem("m_summed"), sem("m_step")
        gu_free = sem("gu_free")
        gated, hid_hi_ok, hid_ok = sem("gated"), sem("hid_hi_ok"), sem("hid_ok")
        x_ok = sem("x_ok")
        block = ctx.enter_context(nc.Block())

        X_AT, n = {}, 2
        for name in NORMS:
            X_AT[name] = n
            n += {"ffn1": 8, "mix": 8, "ffn2": 8, "final": 8, "a": 4, "mlp0": 8, "kv": 0, "b": 4,
                  "mlp1": 8}[name]
        X_END = n

        def load_a(e, stage, c, i=None):
            ca = A_BASE[stage] + c
            slot = ca % 2
            if i is not None or ca >= 2:
                e.wait_ge(a_split, lin(ca - 1, i, 2))
            lo, hi = raw_a[:, slot, 0:1024], raw_a[:, slot, 1024:2048]
            if stage in ("ffn1", "ffn2"):
                n = stage[-1]
                cols = bass.ds(lin(c * P, i, 2 * P), P)
                parts = [(lo.rearrange("p (k n) -> p k n", k=KD), wv["g" + n][:, :, cols]),
                         (hi.rearrange("p (k n) -> p k n", k=KD), wv["u" + n][:, :, cols])]
            elif stage in ("mlp0", "mlp1"):
                cols = bass.ds(lin(c * P, i, 2 * P), P)
                t = lo.rearrange("p (k n) -> p k n", k=KD)
                parts = [(t[:, 0:4, :], wv[stage][:, 0:4, cols]), (t[:, 4:8, :], wv[stage][:, 4:8, cols])]
            elif stage == "glu":
                t = lo.rearrange("p (a k n) -> p a k n", a=2, k=4)
                parts = [(t[:, a], wv["glu"][:, :, (2 * c + a) * P:(2 * c + a + 1) * P]) for a in range(2)]
            elif stage in ("a_v", "b_v"):
                w = wv["a_in"] if stage == "a_v" else wv["kv"]
                parts = [(h, w[:, 2 * c + a, 1024:2048]) for a, h in enumerate((lo, hi))]
            else:
                w, cols = {
                    "w_in": (wv["w_in"], [P * t for t in WIN_TILES]),
                    "w_out": (wv["w_out"], [P * t for t in range(8)]),
                    "a_qk": (wv["a_in"], [P * t for t in range(8)]),
                    "a_g": (wv["a_in"], [2048 + P * t for t in range(8)]),
                    "a_out": (wv["a_out"], [P * t for t in range(8)]),
                    "b_k": (wv["kv"], [P * t for t in range(8)]),
                    "b_q": (wv["b_q"], [P * t for t in range(8)]),
                    "b_out": (wv["b_out"], [P * t for t in range(8)]),
                }[stage]
                parts = [(h.rearrange("p (k n) -> p k n", k=KD), w[:, :, cols[2 * c + a]:cols[2 * c + a] + P])
                         for a, h in enumerate((lo, hi))]
            for dst, src in parts:
                e.dma_start(dst, src).then_inc(a_loaded[slot], 16)

        def load_a_ahead(e, stage, c):
            at = A_BASE[stage] + c + 4
            if at < len(A_ORDER):
                load_a(e, *A_ORDER[at])

        def load_d(e, d, i=None):
            if i is None and d >= D_TOTAL:
                return
            stage = [s for s, _ in D_STAGES if D_BASE[s] <= d][-1]
            slot = d % 2
            if i is not None or d >= 2:
                e.wait_ge(d_split, lin(d - 1, i, 2))
            e.dma_start(raw_d[:, slot, :].unsqueeze(1),
                        dv[stage][:, bass.ds(lin(d - D_BASE[stage], i, 2), 1), :])\
                .then_inc(d_loaded[slot], 16)

        def load_m(e, m, i=None):
            if i is None and m >= NMODC:
                return
            if i is not None or m >= 2:
                e.wait_ge(m_summed, lin(m - 1, i, 2))
            e.dma_start(raw_m[:, m % 2, :, :], wv["mod"][:, :, bass.ds(lin(m * MODC, i, 2 * MODC), MODC)])\
                .then_inc(m_loaded[m % 2], 16)

        @block.sync
        def _(e):
            load_m(e, 0)
            load_m(e, 1)
            for m in range(2, MOD0 + 3):
                if m == 4:
                    load_a(e, "ffn1", 0)
                    load_a(e, "ffn1", 1)
                if m == 6:
                    load_d(e, 0)
                    load_d(e, 1)
                load_m(e, m)
            load_a(e, "ffn1", 2)
            load_a(e, "ffn1", 3)
            load_d(e, 2)

            def feed_forward_loads(stage, n):
                with_mod = stage == "ffn1"
                db = D_BASE[stage]
                with e.Fori(0, (n - 4) // 2) as i:
                    for s in range(2):
                        load_a(e, stage, s + 4, i)
                        load_d(e, db + s + 3, i)
                        if with_mod:
                            load_m(e, MOD0 + 3 + s, i)
                for f in range(n - 4, n):
                    load_a_ahead(e, stage, f)
                    load_d(e, db + f + 3)
                    if with_mod:
                        for m in {n - 4: [29], n - 3: [30, 31, 32], n - 2: [33, 34, 35]}.get(f, []):
                            load_m(e, m)

            for stage, n, _, _ in A_STAGES:
                if stage in D_BASE:
                    feed_forward_loads(stage, n)
                else:
                    for c in range(n):
                        load_a_ahead(e, stage, c)
            e.wait_ge(sem("out_rows"), 4)
            for t in range(2):
                e.dma_start(out[0, t * P:(t + 1) * P, :],
                            arena[:, t * D:(t + 1) * D]).then_inc(sem("stored"), 16)
            e.wait_ge(sem("stored"), 32)

        def hi_split_a(e, ca, i=None, size=None):
            slot = ca % 2
            size = size or A_SIZE[A_ORDER[ca][0]]
            e.wait_ge(a_loaded[slot], lin(32 * (ca // 2 + 1), i, 32))
            if i is not None or ca >= 2:
                e.wait_ge(a_used, lin(ca - 1, i, 2))
            e.activation(hi_a[:, slot, 0:size], raw_a[:, slot, 0:size], ACT.Copy).then_inc(a_hi, 1)

        def lo_split_a(e, ca, i=None, size=None):
            slot = ca % 2
            size = size or A_SIZE[A_ORDER[ca][0]]
            e.wait_ge(a_hi, lin(ca + 1, i, 2))
            e.tensor_tensor(lo_a[:, slot, 0:size], raw_a[:, slot, 0:size],
                            hi_a[:, slot, 0:size].bitcast(F32), ALU.subtract).then_inc(a_split, 1)

        def hi_split_d(e, d, i=None):
            if i is None and d >= D_TOTAL:
                return
            slot = d % 2
            e.wait_ge(d_loaded[slot], lin(16 * (d // 2 + 1), i, 16))
            if i is not None or d >= 2:
                e.wait_ge(d_used, lin(d - 1, i, 2))
            e.activation(hi_d[:, slot, :], raw_d[:, slot, :], ACT.Copy).then_inc(d_hi, 1)

        def lo_split_d(e, d, i=None):
            if i is None and d >= D_TOTAL:
                return
            slot = d % 2
            e.wait_ge(d_hi, lin(d + 1, i, 2))
            e.tensor_tensor(lo_d[:, slot, :], raw_d[:, slot, :],
                            hi_d[:, slot, :].bitcast(F32), ALU.subtract).then_inc(d_split, 1)

        def ahead(split, e, stage, c):
            at = A_BASE[stage] + c + 2
            if at < len(A_ORDER):
                split(e, at)

        def feed_forward_steps(e, n, step):
            step(0, None)
            with e.Fori(0, (n - 4) // 2) as i:
                for s in range(2):
                    step(1 + s, i)
            for f in range(n - 3, n):
                step(f, None)

        def three(e, dst, w_hi, w_lo, r_hi, r_lo, start, stop):
            e.matmul(dst, w_hi, r_hi, start=start, stop=False, skip_group_check=True)
            e.matmul(dst, w_hi, r_lo, start=False, stop=False, skip_group_check=True)
            return e.matmul(dst, w_lo, r_hi, start=False, stop=stop, skip_group_check=True)

        @block.tensor
        def _(e):
            def in_tile(slot, t, dst, kn, first=None):
                for k in range(kn):
                    at = t * kn * P + k * P
                    if first:
                        e.wait_ge(sem("h"), after("h", first, k + 1))
                    mm = three(e, dst, hi_a[:, slot, at:at + P], lo_a[:, slot, at:at + P],
                               h_hi[:, k, :], h_lo[:, k, :], k == 0, k == kn - 1)
                return mm

            def gu_chunk(stage, f, i=None, nt=2, kn=KD, first=None):
                ca, g = A_BASE[stage] + f, GU_BASE[stage] + f
                slot, bank = ca % 2, g % 2
                e.wait_ge(a_split, lin(ca + 1, i, 2))
                if i is not None or g >= 2:
                    e.wait_ge(gu_free, lin(g - 1, i, 2))
                for t in range(nt):
                    mm = in_tile(slot, t, ps[:, bank, t * S:(t + 1) * S], kn, first if t == 0 else None)
                mm.then_inc(a_used, 1)

            def down(stage, f, i=None, last=False):
                d = D_BASE[stage] + f
                slot = d % 2
                e.wait_ge(d_split, lin(d + 1, i, 2))
                e.wait_ge(hid_ok, lin(d + 1, i, 2))
                for t in range(KD):
                    mm = three(e, ps[:, 2 + t // 2, (t % 2) * S:(t % 2 + 1) * S],
                               hi_d[:, slot, t * P:(t + 1) * P], lo_d[:, slot, t * P:(t + 1) * P],
                               hid_hi[:, slot, :], hid_lo[:, slot, :], False, last)
                mm.then_inc(d_used, 1)

            def mod_sum(m, i=None):
                e.wait_ge(m_summed, lin(m + 1, i, 2))
                for t in range(2):
                    mm = e.matmul(ps[:, 7, bass.ds(lin(2 * m + t, i, 4), 1)], acc_m[:, m % 2, t * P:(t + 1) * P],
                                  ones[:, 0:1], start=True, stop=True)
                mm.then_inc(sem("m_done"), 1)

            def feed_forward(stage, n, nt):
                with_mod = stage == "ffn1"
                gu_chunk(stage, 0, None, nt, first=stage)
                clear_acc()
                if with_mod:
                    mod_sum(MOD0)
                with e.Fori(0, (n - 2) // 2) as i:
                    for s in range(2):
                        gu_chunk(stage, 1 + s, i, nt)
                        if with_mod:
                            mod_sum(MOD0 + 1 + s, i)
                        down(stage, s, i)
                gu_chunk(stage, n - 1, None, nt)
                if with_mod:
                    for m in range(MOD0 + n - 1, NMODC - 2):
                        mod_sum(m)
                down(stage, n - 2)
                if with_mod:
                    mod_sum(NMODC - 2)
                    mod_sum(NMODC - 1)
                down(stage, n - 1, None, True)

            def clear_acc():
                e.wait_ge(sem("zero_ok"), 1)
                for b in range(4):
                    e.matmul(ps[:, 2 + b, :], zero_w[:, :], h_hi[:, 0:2, :], start=True, stop=False,
                             skip_group_check=True)

            def sum_squares(name, n, dst=None):
                for k in range(n):
                    if k % 4 == 0:
                        e.wait_ge(sem("sq"), after("sq", name, k // 4 + 1))
                    mm = e.matmul(ps[:, 6, 0:S], ones[:, :], tmp[:, k, :], start=(k == 0), stop=(k == n - 1))
                mm.then_inc(sem("ss"), 1)

            def project(stage, n, first, nt=2, kn=KD):
                for c in range(n):
                    gu_chunk(stage, c, None, nt, kn, first if c == 0 else None)

            def rows_product(stage):
                for c in range(4):
                    ca = A_BASE[stage] + c
                    slot = ca % 2
                    e.wait_ge(a_split, ca + 1)
                    for a in range(2):
                        k = 2 * c + a
                        for t in range(2):
                            hh, hl = h_hi[:, k, t * P:(t + 1) * P], h_lo[:, k, t * P:(t + 1) * P]
                            for half in range(2):
                                at = a * 1024 + half * 512
                                w_hi, w_lo = hi_a[:, slot, at:at + 512], lo_a[:, slot, at:at + 512]
                                dst = ps[:, 2 + 2 * t + half, :]
                                e.matmul(dst, hh, w_hi, start=(k == 0), stop=False, skip_group_check=True)
                                e.matmul(dst, hh, w_lo, start=False, stop=False, skip_group_check=True)
                                mm = e.matmul(dst, hl, w_hi, start=False, stop=(k == 7), skip_group_check=True)
                    mm.then_inc(a_used, 1)

            e.wait_ge(sem("ident_ok"), 1)
            e.wait_ge(sem("ones"), 1)
            e.wait_ge(sem("ld_v0"), 32)
            e.transpose(ps[:, 6, 0:80], v0_rows, ident[0:80, 0:80]).then_inc(sem("t_v0"), 1)
            e.wait_ge(sem("ld_x"), 16)
            for k in range(KD):
                for t in range(2):
                    mm = e.transpose(ps[:, 2 + k // 2, (k % 2) * S + t * P:(k % 2) * S + (t + 1) * P],
                                     arena[:, t * D + k * P:t * D + (k + 1) * P], ident[:, :])
            mm.then_inc(sem("t_x"), 1)
            e.wait_ge(sem("ld_v1"), 16 * len(V1_ROWS))
            e.transpose(ps[:, 0, 0:V1_N], v1_rows, ident[0:V1_N, 0:V1_N]).then_inc(sem("t_v1"), 1)
            e.wait_ge(sem("ld_v2"), 16 * 6)
            e.transpose(ps[:, 1, 0:V2_N], v2_rows, ident[0:V2_N, 0:V2_N]).then_inc(sem("t_v2"), 1)
            e.wait_ge(sem("v0_ok"), 1)
            sum_squares("ffn1", KD)
            for m in range(MOD0):
                mod_sum(m)
            e.wait_ge(x_ok, 2)
            e.wait_ge(sem("v12_ok"), 2)
            feed_forward("ffn1", NF, 2)

            e.wait_ge(sem("b_bd_ok"), 1)
            e.wait_ge(sem("ld_c"), 16 * 16)
            for q, (src, bank) in enumerate(((b_bd, 6), (b_bd, 0), (c_in, 1), (c_in, 6))):
                if q == 3:
                    e.wait_ge(sem("bc_t_ok"), 1)
                for u in range(4):
                    if q < 2:
                        part = b_bd[:, q, 4 * u:4 * u + 4, :].rearrange("p t c -> p (t c)")
                    else:
                        part = c_in[:, q - 2, u, :]
                    mm = e.transpose(ps[:, bank, u * P:(u + 1) * P], part, ident[:, :])
                mm.then_inc(sem("bc_t"), 1)
            e.wait_ge(sem("bc_t_ok"), 5)
            sum_squares("mix", KD)

            def ssm_inputs(u):
                if u >= 1:
                    e.wait_ge(sem("bu_read"), u)
                for half in range(2):
                    if half == 1:
                        e.wait_ge(sem("bu_half"), u + 1)
                    for r in range(2):
                        for j in (half, half + 2):
                            rows = slice(32 * j, 32 * j + 32)
                            mm = e.matmul(ps[:, 2 + 2 * r + j // 2, (j % 2) * S:(j % 2 + 1) * S],
                                          b_t[rows, r, u, :], proj[rows, 12 + u, :], start=True, stop=True,
                                          skip_group_check=True)
                    mm.then_inc(sem("bu" if half else "bu_half"), 1)

            def ssm_outputs(u):
                e.wait_ge(sem("remod"), 4 * (u + 1))
                if u >= 1:
                    e.wait_ge(sem("y_pre"), u)
                for j in range(4):
                    rows = slice(32 * j, 32 * j + 32)
                    for q, which in enumerate((0, 1, 2, 2)):
                        mm = e.matmul(ps[rows, 6, 0:S], c_t[:, which, u, rows], prod[q][:, j * S:(j + 1) * S],
                                      start=(q == 0), stop=(q == 3), skip_group_check=True)
                mm.then_inc(sem("y_ssm"), 1)

            for c in range(8):
                gu_chunk("w_in", c, first="mix" if c == 0 else None)
                if c % 2 == 1:
                    u = c // 2
                    e.wait_ge(gu_free, GU_BASE["w_in"] + 2)
                    ssm_inputs(u)
                    if u >= 1:
                        ssm_outputs(u - 1)
            ssm_outputs(3)
            sum_squares("conv", 4)
            for c in range(2):
                gu_chunk("glu", c, None, 2, 4, "glu" if c == 0 else None)
            e.wait_ge(sem("root"), after("root", "conv", 1))
            sum_squares("ssm", 4)
            project("w_out", 4, "ymix")
            sum_squares("ffn2", KD)
            feed_forward("ffn2", NF, 2)
            sum_squares("final", KD)

            sum_squares("a", KD)
            e.wait_ge(sem("t"), after("t", "a", KD))
            e.wait_ge(sem("ld_att"), 16 * 3)
            e.wait_ge(sem("root"), after("root", "a", 1))
            for k in range(KD):
                mm = e.matmul(ps[0:16, 6, 0:S], zw[:, k, :], tmp[:, k, :], start=(k == 0), stop=(k == KD - 1))
            mm.then_inc(sem("z"), 1)
            e.wait_ge(sem("z_ok"), 1)
            for h in range(GH):
                mm = e.matmul(ps[:, 2 + h // 2, (h % 2) * S:(h % 2 + 1) * S], gup[:, h * P:(h + 1) * P],
                              z_sb[:, :], start=True, stop=True, skip_group_check=True)
            mm.then_inc(sem("gate_in"), 1)
            project("a_qk", 4, "a")
            e.wait_ge(sem("gate_read"), 2)
            rows_product("a_v")
            project("a_g", 4, None)
            e.wait_ge(sem("qdec"), 1)
            e.wait_ge(sem("v_rows_a"), 1)
            off = 0
            for b in range(NBLK):
                n = GBLK * (b + 1)
                e.wait_ge(sem("kdec"), b + 1)
                for h in range(GH):
                    for jt in range(1 + (b >= 4)):
                        m = min(P, n - jt * P)
                        at = off + h * n + jt * P
                        mm = e.matmul(ps[0:m, 2 + 2 * jt + h // 2, (h % 2) * S + b * GBLK:(h % 2) * S + (b + 1) * GBLK],
                                      k_dec[:, at:at + m], q_dec[:, h * S + b * GBLK:h * S + (b + 1) * GBLK],
                                      start=True, stop=True, skip_group_check=True)
                off += GH * n
            mm.then_inc(sem("att"), 1)
            e.wait_ge(sem("at_sb"), 9)
            for h in range(GH):
                for vh in range(2):
                    t = 2 * h + vh
                    dst = ps[:, 2 + t // 2, (t % 2) * S:(t % 2 + 1) * S]
                    cols = slice(h * GDV + vh * P, h * GDV + (vh + 1) * P)
                    e.matmul(dst, v_rows[:, 0, cols], at_sb[:, h * S:(h + 1) * S], start=True, stop=False,
                             skip_group_check=True)
                    mm = e.matmul(dst[:, P:S], v_rows[:, 1, cols], at_sb[:, 1024 + h * S + P:1024 + (h + 1) * S],
                                  start=False, stop=True, skip_group_check=True)
            mm.then_inc(sem("o_a"), 1)
            e.wait_ge(sem("osq_a"), 1)
            for h in range(GH):
                for vh in range(2):
                    mm = e.matmul(ps[:, 6 + h // 2, (h % 2) * S:(h % 2 + 1) * S], ones[:, :],
                                  k_dec[:, (2 * h + vh) * S:(2 * h + vh + 1) * S], start=(vh == 0), stop=(vh == 1),
                                  skip_group_check=True)
            mm.then_inc(sem("oss_a"), 1)
            project("a_out", 4, "oa")
            sum_squares("mlp0", KD)
            feed_forward("mlp0", NHID, 1)

            sum_squares("kv", KD)
            project("b_k", 4, "kv")
            rows_product("b_v")
            project("b_q", 4, "b")

            def head_squares(name, w, src, banks, h0, nh):
                for h in range(nh):
                    mm = e.matmul(ps[:, banks + h // 2, (h % 2) * S:(h % 2 + 1) * S], w[:, :],
                                  src[:, h0 + h, :], start=True, stop=True, skip_group_check=True)
                mm.then_inc(sem(name), 1)

            e.wait_ge(sem("v_rows_b"), 1)
            e.wait_ge(sem("ksq"), 1)
            e.wait_ge(sem("masks"), 5)
            head_squares("kss", ones_blk, tmp, 2, 0, 8)
            e.wait_ge(sem("kroot"), 1)
            e.wait_ge(sem("qsq"), 1)
            head_squares("qss", ones_blk, tiles(area(6144, 2048)), 2, 0, 8)
            e.wait_ge(sem("k_n"), 1)
            e.wait_ge(sem("q_n"), 1)

            def scores(h):
                b = 0 if h % 2 == 0 else 6
                if h >= 2:
                    e.wait_ge(sem("s_read"), h - 1)
                    e.wait_ge(sem("a_t"), h - 1)
                for c in range(2):
                    rows = slice(DD * c, DD * c + DD)
                    e.matmul(ps[:, b + c, 0:P], q_n[rows, h, 0:P], k_n[rows, h, 0:P], start=True, stop=True,
                             skip_group_check=True)
                    mm = e.matmul(ps[:, b + c, P:P + S], q_n[rows, h, P:S], k_n[rows, h, 0:S], start=True,
                                  stop=True, skip_group_check=True)
                mm.then_inc(sem("scores"), 1)

            def weigh(h):
                b = 0 if h % 2 == 0 else 6
                at = (h % 2) * 384
                e.wait_ge(sem("a_ok"), 2 * (h + 1))
                for q in range(3):
                    mm = e.transpose(ps[:, b, q * P:(q + 1) * P], a_sb[:, at + q * P:at + (q + 1) * P], ident[:, :])
                mm.then_inc(sem("a_turned"), 1)
                e.wait_ge(sem("a_t"), h + 1)
                dst = ps[:, 2 + h // 2, (h % 2) * S:(h % 2 + 1) * S]
                e.matmul(dst, v_rows[:, 0, h * P:(h + 1) * P], a_t[:, at:at + S], start=True, stop=False,
                         skip_group_check=True)
                e.matmul(dst[:, P:S], v_rows[:, 1, h * P:(h + 1) * P], a_t[:, at + S:at + S + P], start=False,
                         stop=True, skip_group_check=True).then_inc(sem("o_b"), 1)

            scores(0)
            for h in range(DH):
                if h + 1 < DH:
                    scores(h + 1)
                weigh(h)
            for half in range(2):
                e.wait_ge(sem("osq_b"), half + 1)
                head_squares("oss_b", ones, tmp, 6 if half == 0 else 0, 4 * half, 4)
            project("b_out", 4, "ob")
            sum_squares("mlp1", KD)
            feed_forward("mlp1", NHID, 1)
            for t in range(2):
                for k in range(KD):
                    if t == 0:
                        e.wait_ge(x_ok, X_AT["mlp1"] + k + 1)
                    bank = (6 + k // 4) if t == 0 else k // 4
                    mm = e.transpose(ps[:, bank, (k % 4) * P:(k % 4 + 1) * P], x_t[:, k, t * P:(t + 1) * P], ident[:, :])
                    if k % 4 == 3:
                        mm.then_inc(sem("x_turned"), 1)

        @block.scalar
        def _(e):
            def act(dst, src, f, **kw):
                return e.activation(dst, src, f, **kw)

            def squares(name, src, n, wait=None):
                for q in range((n + 3) // 4):
                    if wait:
                        wait(q)
                    act(tmp[:, 4 * q:4 * q + 4, :], src[:, 4 * q:4 * q + 4, :], ACT.Square)\
                        .then_inc(sem("sq"), 1)

            def roots(name, n):
                e.wait_ge(sem("ss"), after("ss", name, 1))
                act(root[:, 0, :], ps[:, 6, 0:S], ACT.Sqrt, scale=1.0 / n, bias=eps[:, 0:1])\
                    .then_inc(sem("root"), 1)

            def h_his(name, src, n, shift=None):
                for k in range(n):
                    e.wait_ge(sem("t"), after("t", name, k + 1))
                    if shift is None:
                        act(h_hi[:, k, :], src[:, k, :], ACT.Copy).then_inc(sem("hh"), 1)
                    else:
                        act(h_hi[:, k, :], src[:, k, :], ACT.Identity, bias=shift(k)).then_inc(sem("hh"), 1)

            def norm(name, shift=None):
                e.wait_ge(x_ok, X_AT[name])
                squares(name, x_t, KD)
                roots(name, D)
                h_his(name, tmp, KD, shift)

            def feed_forward(stage, n):
                f1 = ACT.Silu if stage.startswith("ffn") else ACT.Relu
                ab, db, gb = A_BASE[stage], D_BASE[stage], GU_BASE[stage]

                def step(f, i):
                    slot = (db + f) % 2
                    e.wait_ge(a_used, lin(ab + f + 1, i, 2))
                    if i is not None or db + f >= 2:
                        e.wait_ge(gu_free, lin(gb + f - 1, i, 2))
                    act(gate[:, slot, :], ps[:, (gb + f) % 2, 0:S], f1).then_inc(gated, 1)
                    if i is not None:
                        hi_split_a(e, ab + f + 2, i, A_SIZE[stage])
                    else:
                        ahead(hi_split_a, e, stage, f)
                    e.wait_ge(gu_free, lin(gb + f + 1, i, 2))
                    if i is not None or db + f >= 2:
                        e.wait_ge(d_used, lin(db + f - 1, i, 2))
                    act(hid_hi[:, slot, :], hid[:, slot, :], ACT.Copy).then_inc(hid_hi_ok, 1)
                    if i is not None or f >= 1:
                        hi_split_d(e, db + f + 1, i)

                feed_forward_steps(e, n, step)
                hi_split_d(e, db + n + 1)

            e.dma_start(v0_rows[0:72, :], T["b_mod"][0].rearrange("(r c) -> r c", c=P)).then_inc(sem("ld_v0"), 16)
            e.dma_start(v0_rows[72:80, :], T["cond"][0].rearrange("(r c) -> r c", c=P)).then_inc(sem("ld_v0"), 16)
            e.dma_start(arena[:, 0:2 * D].rearrange("p (t n) -> p t n", t=2),
                        T["x"][0].rearrange("(t p) n -> p t n", p=P)).then_inc(sem("ld_x"), 16)
            e.wait_ge(sem("t_v0"), 1)
            act(cact[:, :], ps[:, 6, 72:80], ACT.Silu).then_inc(sem("cact"), 1)
            act(v0[:, :], ps[:, 6, 0:80], ACT.Copy).then_inc(sem("v0_ok"), 1)
            e.wait_ge(sem("t_x"), 1)
            for q in range(2):
                act(x_t[:, 4 * q:4 * q + 4, :], acc4[:, 1024 * q:1024 * (q + 1)], ACT.Copy).then_inc(x_ok, 1)
            e.wait_ge(sem("eps_ok"), 1)
            e.wait_ge(x_ok, 2)
            squares("ffn1", x_t, KD)
            roots("ffn1", D)
            hi_split_a(e, 0)
            hi_split_a(e, 1)
            hi_split_d(e, 0)
            hi_split_d(e, 1)
            e.wait_ge(sem("t_v1"), 1)
            act(v1[:, :], ps[:, 0, 0:V1_N], ACT.Copy).then_inc(sem("v12_ok"), 1)
            e.wait_ge(sem("t_v2"), 1)
            act(v2[:, :], ps[:, 1, 0:V2_N], ACT.Copy).then_inc(sem("v12_ok"), 1)
            e.wait_ge(sem("ld_dt"), 32)
            act(dt_col[:, :], dt_col[:, :], ACT.Exp).then_inc(sem("dt"), 1)
            e.wait_ge(sem("s5_args"), 1)
            act(s5[:, 2, :], s5[:, 0, :], ACT.Exp).then_inc(sem("s5_mag"), 1)
            e.wait_ge(sem("s5_red"), 2)
            act(s5[:, 3, :], s5[:, 6, :], ACT.Sin).then_inc(sem("s5_trig"), 1)
            act(s5[:, 4, :], s5[:, 7, :], ACT.Sin).then_inc(sem("s5_trig"), 1)
            h_his("ffn1", tmp, KD, lambda k: mod[:, k:k + 1])
            feed_forward("ffn1", NF)

            for q, (dst, bank, scale) in enumerate(((b_t[:, 0], 6, 1.0), (b_t[:, 1], 0, 1.0), (c_t[:, 0], 1, 1.0),
                                                    (c_t[:, 1], 1, -1.0), (c_t[:, 2], 6, -1.0))):
                e.wait_ge(sem("bc_t"), (1, 2, 3, 3, 4)[q])
                act(dst, ps[:, bank, :].rearrange("p (u n) -> p u n", u=4), ACT.Copy, scale=scale)\
                    .then_inc(sem("bc_t_ok"), 1)
            norm("mix", lambda k: mod[:, 3 * KD + k:3 * KD + k + 1])
            for c in range(8):
                e.wait_ge(a_used, A_BASE["w_in"] + c + 1)
                t0 = WIN_TILES[2 * c]
                act(proj[:, t0:t0 + 2, :], ps[:, (GU_BASE["w_in"] + c) % 2, :], ACT.Copy).then_inc(gu_free, 1)
                ahead(hi_split_a, e, "w_in", c)
            for u in range(4):
                e.wait_ge(sem("y_pre"), u + 1)
                act(y_ssm[:, u, :], y_ssm[:, u, :], ACT.Gelu_apprx_tanh).then_inc(sem("gelu"), 1)
                e.wait_ge(sem("gelu"), u + 1)
                act(h_hi[:, u, :], y_ssm[:, u, :], ACT.Copy).then_inc(sem("hh"), 1)
            e.wait_ge(sem("conv_ok"), 7)
            squares("conv", proj[:, 0:4, :], 4)
            roots("conv", 512)
            for c in range(2):
                e.wait_ge(a_used, A_BASE["glu"] + c + 1)
                for a in range(2):
                    t = 2 * c + a
                    ins = act(proj[:, 12 + t, :], ps[:, (GU_BASE["glu"] + c) % 2, a * S:(a + 1) * S], ACT.Sigmoid,
                              bias=vec(v1, V1, "glu_b", t))
                ins.then_inc(gu_free, 1)
                ahead(hi_split_a, e, "glu", c)
            e.wait_ge(sem("glu_ok"), 1)
            act(tmp[:, 0:4, :], y_ssm, ACT.Square).then_inc(sem("sq"), 1)
            e.wait_ge(sem("ss"), after("ss", "ssm", 1))
            act(root[:, 1, :], ps[:, 6, 0:S], ACT.Sqrt, scale=1.0 / 512, bias=eps[:, 0:1]).then_inc(sem("root"), 1)
            h_his("ymix", tmp, KD)
            for c in range(4):
                e.wait_ge(a_used, A_BASE["w_out"] + c + 1)
                ahead(hi_split_a, e, "w_out", c)
            norm("ffn2", lambda k: mod[:, 6 * KD + k:6 * KD + k + 1])
            feed_forward("ffn2", NF)
            e.wait_ge(x_ok, X_AT["final"])
            squares("final", x_t, KD)
            roots("final", D)

            norm("a")
            e.wait_ge(sem("z"), 1)
            act(z_sb[:, :], ps[0:16, 6, 0:S], ACT.Copy).then_inc(sem("z_ok"), 1)
            e.wait_ge(sem("gate_in"), 1)
            mag = area(8192, 1024)
            for h in range(GH):
                ins = act(mag[:, h * S:(h + 1) * S], acc4[:, h * S:(h + 1) * S], ACT.Abs,
                          bias=vec(v1, V1, "a_b_gate_2", h))
            ins.then_inc(sem("gate_read"), 1)
            e.wait_ge(sem("gate_read"), 1)
            act(mag, mag, ACT.Exp, scale=-1.0).then_inc(sem("gate_exp"), 1)
            e.wait_ge(sem("gate_exp"), 1)
            act(mag, mag, ACT.Ln, bias=1.0).then_inc(sem("gate_ln"), 1)
            for c in range(4):
                e.wait_ge(a_used, A_BASE["a_qk"] + c + 1)
                act(qk[:, 2 * c:2 * c + 2, :], ps[:, (GU_BASE["a_qk"] + c) % 2, :], ACT.Copy).then_inc(gu_free, 1)
                ahead(hi_split_a, e, "a_qk", c)
            e.wait_ge(sem("q_arg"), 1)
            act(q_dec, q_dec, ACT.Exp, scale=1.0 / TAU).then_inc(sem("q_exp"), 1)
            for c in range(4):
                e.wait_ge(a_used, A_BASE["a_v"] + c + 1)
                ahead(hi_split_a, e, "a_v", c)
            for t in range(2):
                ins = act(v_rows[:, t, :], acc4[:, t * 1024:(t + 1) * 1024], ACT.Copy)
            ins.then_inc(sem("v_rows_a"), 1)
            off = 0
            for b in range(NBLK):
                n = GH * GBLK * (b + 1)
                e.wait_ge(sem("k_arg"), b + 1)
                act(k_dec[:, off:off + n], k_dec[:, off:off + n], ACT.Exp, scale=1.0 / TAU).then_inc(sem("k_exp"), 1)
                off += n
            for c in range(4):
                e.wait_ge(a_used, A_BASE["a_g"] + c + 1)
                act(silu_g[:, 2 * c:2 * c + 2, :], ps[:, (GU_BASE["a_g"] + c) % 2, :], ACT.Silu).then_inc(gu_free, 1)
                ahead(hi_split_a, e, "a_g", c)
            e.wait_ge(sem("o_a"), 1)
            act(k_dec[:, 0:2048], acc4, ACT.Square).then_inc(sem("osq_a"), 1)
            e.wait_ge(sem("oss_a"), 1)
            act(k_dec[:, 2048:3072], psf[:, 3072:4096], ACT.Sqrt, scale=1.0 / GDV, bias=eps[:, 0:1])\
                .then_inc(sem("oroot_a"), 1)
            h_his("oa", tmp, KD)
            for c in range(4):
                e.wait_ge(a_used, A_BASE["a_out"] + c + 1)
                ahead(hi_split_a, e, "a_out", c)
            norm("mlp0")
            feed_forward("mlp0", NHID)

            norm("kv")
            for c in range(4):
                e.wait_ge(a_used, A_BASE["b_k"] + c + 1)
                act(k_n[:, 2 * c:2 * c + 2, :], ps[:, (GU_BASE["b_k"] + c) % 2, :], ACT.Copy).then_inc(gu_free, 1)
                ahead(hi_split_a, e, "b_k", c)
            for c in range(4):
                e.wait_ge(a_used, A_BASE["b_v"] + c + 1)
                ahead(hi_split_a, e, "b_v", c)
            for t in range(2):
                ins = act(v_rows[:, t, :], acc4[:, t * 1024:(t + 1) * 1024], ACT.Copy)
            ins.then_inc(sem("v_rows_b"), 1)
            h_his("b", tmp, KD)
            e.wait_ge(sem("h"), after("h", "b", KD))
            act(tmp_flat, area(0, 2048), ACT.Square).then_inc(sem("ksq"), 1)
            for c in range(4):
                e.wait_ge(a_used, A_BASE["b_q"] + c + 1)
                act(q_n[:, 2 * c:2 * c + 2, :], ps[:, (GU_BASE["b_q"] + c) % 2, :], ACT.Copy).then_inc(gu_free, 1)
                ahead(hi_split_a, e, "b_q", c)
            e.wait_ge(gu_free, GU_BASE["b_q"] + 4)
            act(area(6144, 2048), area(4096, 2048), ACT.Square).then_inc(sem("qsq"), 1)
            e.wait_ge(sem("kss"), 1)
            act(tmp_flat, acc4, ACT.Sqrt, scale=1.0 / DD, bias=eps[:, 0:1]).then_inc(sem("kroot"), 1)
            e.wait_ge(sem("qss"), 1)
            act(area(6144, 2048), acc4, ACT.Sqrt, scale=1.0 / DD, bias=eps[:, 0:1]).then_inc(sem("qroot"), 1)
            e.wait_ge(sem("lam_dots"), 1)
            act(lam_s[:, 2:4], lam_s[:, 0:2], ACT.Exp).then_inc(sem("lam_exp"), 1)
            for h in range(DH):
                hb = h % 2
                e.wait_ge(sem("s_max"), 2 * (h + 1))
                for c in range(2):
                    for q in range(2):
                        at = hb * 768 + c * 384 + (P if q else 0)
                        n = S if q else P
                        ins = act(p_sb[:, at:at + n], s_sb[:, at:at + n], ACT.Exp,
                                  bias=st_s[:, hb, 2 * q + c:2 * q + c + 1],
                                  accum_out=st_s[:, hb, 4 + 2 * q + c:5 + 2 * q + c])
                        ins.then_inc(sem("p_exp"), 1)
            for half in range(2):
                e.wait_ge(sem("o_b"), 4 * (half + 1))
                if half == 0:
                    e.wait_ge(sem("q_n"), 1)
                act(tmp_flat[:, half * 1024:(half + 1) * 1024], acc4[:, half * 1024:(half + 1) * 1024], ACT.Square)\
                    .then_inc(sem("osq_b"), 1)
            for half in range(2):
                e.wait_ge(sem("oss_b"), half + 1)
                src = psf[:, 3072:4096] if half == 0 else psf[:, 0:1024]
                act(area(6144 + half * 1024, 1024), src, ACT.Sqrt, scale=1.0 / P, bias=eps[:, 0:1])\
                    .then_inc(sem("oroot_b"), 1)
            h_his("ob", tmp, KD)
            for c in range(4):
                e.wait_ge(a_used, A_BASE["b_out"] + c + 1)
                ahead(hi_split_a, e, "b_out", c)
            norm("mlp1")
            feed_forward("mlp1", NHID)
            for t in range(2):
                for q in range(2):
                    if (2 * t + q) % 2 == 0:
                        e.wait_ge(sem("x_turned"), 2 * t + q + 1)
                        bank = (6 + q) if t == 0 else q
                        act(arena[:, t * D + q * 512:t * D + (q + 1) * 512], ps[:, bank, :], ACT.Copy)\
                            .then_inc(sem("out_rows"), 1)

        @block.vector
        def _(e):
            def h_los(name, src, n, shift=None):
                for k in range(n):
                    e.wait_ge(sem("hh"), after("hh", name, k + 1))
                    hi = h_hi[:, k, :].bitcast(F32)
                    if shift is None:
                        ins = e.tensor_tensor(h_lo[:, k, :], src[:, k, :], hi, ALU.subtract)
                    else:
                        ins = e.scalar_tensor_tensor(out=h_lo[:, k, :], in0=src[:, k, :], scalar=shift(k), in1=hi,
                                                     op0=ALU.add, op1=ALU.subtract)
                    ins.then_inc(sem("h"), 1)

            def rstds(name):
                e.wait_ge(sem("root"), after("root", name, 1))
                e.reciprocal(rstd[:, 0, :], root[:, 0, :]).then_inc(sem("rstd"), 1)
                e.wait_ge(sem("rstd"), after("rstd", name, 1))

            def scaled(name, scale):
                for k in range(KD):
                    e.scalar_tensor_tensor(out=tmp[:, k, :], in0=x_t[:, k, :], scalar=scale(k), in1=rstd[:, 0, :],
                                           op0=ALU.mult, op1=ALU.mult).then_inc(sem("t"), 1)

            def norm(name, scale, shift=None):
                rstds(name)
                scaled(name, scale)
                h_los(name, tmp, KD, shift)

            def mod_chunk(m, i=None):
                slot = m % 2
                e.wait_ge(m_loaded[slot], lin(16 * (m // 2 + 1), i, 16))
                if i is not None or m >= 2:
                    e.wait_ge(sem("m_done"), lin(m - 1, i, 2))
                for k in range(KD):
                    if k == 0:
                        ins = e.tensor_scalar(acc_m[:, slot, :], raw_m[:, slot, k, :], cact[:, k:k + 1], None, ALU.mult)
                    else:
                        e.wait_ge(m_step, lin(7 * m + k, i, 14))
                        ins = e.scalar_tensor_tensor(out=acc_m[:, slot, :], in0=raw_m[:, slot, k, :],
                                                     scalar=cact[:, k:k + 1], in1=acc_m[:, slot, :],
                                                     op0=ALU.mult, op1=ALU.add)
                    if k < KD - 1:
                        ins.then_inc(m_step, 1)
                ins.then_inc(m_summed, 1)

            def mod_columns(lo, hi, chunks, name):
                e.wait_ge(sem("m_done"), chunks)
                e.wait_ge(sem("v0_ok"), 1)
                e.tensor_tensor(mod[:, lo:hi], ps[:, 7, lo:hi], v0[:, lo:hi], ALU.add).then_inc(sem(name), 1)
                e.wait_ge(sem(name), 1)

            def norm_scale(n, section, gain):
                e.scalar_tensor_tensor(out=nscale[:, n, :], in0=mod[:, section * KD:(section + 1) * KD], scalar=1.0,
                                       in1=vec(v1, V1, gain, 0, KD), op0=ALU.add, op1=ALU.mult)\
                    .then_inc(sem(f"nscale{n}"), 1)
                e.wait_ge(sem(f"nscale{n}"), 1)

            def feed_forward(stage, n):
                ab, db, gb = A_BASE[stage], D_BASE[stage], GU_BASE[stage]
                up = S if stage.startswith("ffn") else 0

                def step(f, i):
                    slot = (db + f) % 2
                    e.wait_ge(gated, lin(db + f + 1, i, 2))
                    e.tensor_tensor(hid[:, slot, :], gate[:, slot, :], ps[:, (gb + f) % 2, up:up + S], ALU.mult)\
                        .then_inc(gu_free, 1)
                    if i is not None:
                        lo_split_a(e, ab + f + 2, i, A_SIZE[stage])
                    else:
                        ahead(lo_split_a, e, stage, f)
                    e.wait_ge(hid_hi_ok, lin(db + f + 1, i, 2))
                    e.tensor_tensor(hid_lo[:, slot, :], hid[:, slot, :], hid_hi[:, slot, :].bitcast(F32), ALU.subtract)\
                        .then_inc(hid_ok, 1)
                    if i is not None or f >= 1:
                        lo_split_d(e, db + f + 1, i)
                    if stage == "ffn1":
                        for m in MOD_TAIL.get(f, [MOD0 + 1 + f]) if i is None else [MOD0 + 1 + f]:
                            mod_chunk(m, i)

                feed_forward_steps(e, n, step)

            def add_down(stage, scale=None):
                e.wait_ge(d_used, D_BASE[stage] + A_LEN[stage])
                for k in range(KD):
                    src = acc4[:, k * S:(k + 1) * S]
                    if scale is None:
                        ins = e.tensor_tensor(x_t[:, k, :], x_t[:, k, :], src, ALU.add)
                    else:
                        ins = e.scalar_tensor_tensor(out=x_t[:, k, :], in0=src, scalar=scale(k), in1=x_t[:, k, :],
                                                     op0=ALU.mult, op1=ALU.add)
                    ins.then_inc(x_ok, 1)
                lo_split_d(e, D_BASE[stage] + A_LEN[stage] + 1)

            e.memset(zero_w[:, :].bitcast(F32), 0.0).then_inc(sem("zero_ok"), 1)
            e.memset(eps[:, :], EPS).then_inc(sem("eps_ok"), 1)
            e.wait_ge(sem("cact"), 1)
            for m in range(MOD0):
                mod_chunk(m)
                if m == 3:
                    lo_split_a(e, 0)
                    lo_split_a(e, 1)
                if m == 5:
                    lo_split_d(e, 0)
                    lo_split_d(e, 1)
            e.wait_ge(sem("v12_ok"), 2)
            e.wait_ge(sem("dt"), 1)
            c5 = [0]

            def s5_step(ins):
                c5[0] += 1
                ins.then_inc(sem("s5_step"), 1)
                e.wait_ge(sem("s5_step"), c5[0])

            lre, lim = vec(v2, V2, "lambda_re", 0, ST), vec(v2, V2, "lambda_im", 0, ST)
            s5_step(e.tensor_tensor(s5[:, 0, :], lre, dt_col[:, :], ALU.mult))
            e.tensor_tensor(s5[:, 1, :], lim, dt_col[:, :], ALU.mult).then_inc(sem("s5_args"), 1)
            e.wait_ge(sem("s5_args"), 1)
            for row, shift in ((6, 0.25), (7, 0.0)):
                s5_step(e.tensor_scalar(s5[:, 5, :], s5[:, 1, :], 1.0 / (2 * math.pi), shift, ALU.mult, ALU.add))
                s5_step(e.tensor_scalar(s5[:, 5, :], s5[:, 5, :], ROUND, ROUND, ALU.add, ALU.subtract))
                s5_step(e.scalar_tensor_tensor(out=s5[:, row, :], in0=s5[:, 5, :], scalar=-6.28125, in1=s5[:, 1, :],
                                               op0=ALU.mult, op1=ALU.add))
                rest = 2 * math.pi - 6.28125
                s5_step(e.scalar_tensor_tensor(out=s5[:, row, :], in0=s5[:, 5, :], scalar=-rest, in1=s5[:, row, :],
                                               op0=ALU.mult, op1=ALU.add))
                s5_step(e.tensor_scalar(s5[:, row, :], s5[:, row, :], 2 * math.pi * shift, 3.1415925, ALU.add, ALU.min))
                e.tensor_scalar(s5[:, row, :], s5[:, row, :], -3.1415925, None, ALU.max).then_inc(sem("s5_red"), 1)
                e.wait_ge(sem("s5_red"), 1 if row == 6 else 2)
            mod_columns(0, 2 * KD, MOD0, "mod_a")
            norm_scale(0, 1, "ffn1_norm")
            norm("ffn1", lambda k: nscale[:, 0, k:k + 1], lambda k: mod[:, k:k + 1])
            mod_chunk(MOD0)
            e.wait_ge(sem("s5_trig"), 2)
            e.wait_ge(sem("s5_mag"), 1)
            s5_step(e.tensor_tensor(s5[:, 10, :], s5[:, 2, :], s5[:, 3, :], ALU.mult))
            s5_step(e.tensor_tensor(s5[:, 11, :], s5[:, 2, :], s5[:, 4, :], ALU.mult))
            s5_step(e.tensor_scalar(s5[:, 10, :], s5[:, 10, :], -1.0, None, ALU.add))
            s5_step(e.tensor_tensor(s5[:, 12, :], lre, lre, ALU.mult))
            s5_step(e.tensor_tensor(s5[:, 13, :], lim, lim, ALU.mult))
            s5_step(e.tensor_tensor(s5[:, 12, :], s5[:, 12, :], s5[:, 13, :], ALU.add))
            s5_step(e.reciprocal(s5[:, 12, :], s5[:, 12, :]))
            s5_step(e.tensor_tensor(s5[:, 8, :], s5[:, 10, :], lre, ALU.mult))
            s5_step(e.tensor_tensor(s5[:, 13, :], s5[:, 11, :], lim, ALU.mult))
            s5_step(e.tensor_tensor(s5[:, 8, :], s5[:, 8, :], s5[:, 13, :], ALU.add))
            s5_step(e.tensor_tensor(s5[:, 8, :], s5[:, 8, :], s5[:, 12, :], ALU.mult))
            s5_step(e.tensor_tensor(s5[:, 9, :], s5[:, 11, :], lre, ALU.mult))
            s5_step(e.tensor_tensor(s5[:, 13, :], s5[:, 10, :], lim, ALU.mult))
            s5_step(e.tensor_tensor(s5[:, 9, :], s5[:, 9, :], s5[:, 13, :], ALU.subtract))
            e.tensor_tensor(s5[:, 9, :], s5[:, 9, :], s5[:, 12, :], ALU.mult).then_inc(sem("s5_quot"), 1)
            feed_forward("ffn1", NF)
            mod_columns(2 * KD, N_MOD * KD, NMODC, "mod_b")
            e.tensor_scalar(ghalf[:, 0, :], mod[:, 2 * KD:3 * KD], 0.5, None, ALU.mult).then_inc(sem("ghalf0"), 1)
            e.wait_ge(sem("ghalf0"), 1)
            add_down("ffn1", lambda k: ghalf[:, 0, k:k + 1])

            norm_scale(1, 4, "mix_norm")
            norm("mix", lambda k: nscale[:, 1, k:k + 1], lambda k: mod[:, 3 * KD + k:3 * KD + k + 1])
            e.tensor_scalar(ghalf[:, 1, :], mod[:, 8 * KD:9 * KD], 0.5, None, ALU.mult).then_inc(sem("ghalf1"), 1)
            ahead(lo_split_a, e, "w_in", 0)
            ahead(lo_split_a, e, "w_in", 1)
            e.wait_ge(sem("b_bd_ok"), 1)
            bu_re, bu_im = acc4[:, 0:1024], acc4[:, 1024:2048]

            def states(u):
                pr = ph_re[:, 4 * u:4 * u + 4, :].rearrange("p t n -> p (t n)")
                pi = ph_im[:, 4 * u:4 * u + 4, :].rearrange("p t n -> p (t n)")
                e.wait_ge(sem("bu"), u + 1)
                if u >= 1:
                    e.wait_ge(sem("y_ssm"), u)
                for q, (b, f) in enumerate(((bu_re, pr), (bu_im, pi), (bu_im, pr), (bu_re, pi))):
                    ins = e.tensor_tensor(prod[q], b, f, ALU.mult)
                ins.then_inc(sem("bu_read"), 1)
                e.wait_ge(sem("bu_read"), u + 1)
                e.tensor_tensor(w_re, prod[0], prod[1], ALU.add)
                e.tensor_tensor(w_im, prod[2], prod[3], ALU.subtract).then_inc(sem("demod"), 1)
                e.wait_ge(sem("demod"), u + 1)
                for w in (w_re, w_im):
                    for j in range(4):
                        part = w[:, j * S:(j + 1) * S]
                        ins = e.tensor_tensor_scan(part, s5[:, 2, 4 * u + j:4 * u + j + 1].to_broadcast([P, S]), part,
                                                   0.0, ALU.mult, ALU.add)
                ins.then_inc(sem("scanned"), 1)
                e.wait_ge(sem("scanned"), u + 1)
                for q, (f, w) in enumerate(((pr, w_re), (pi, w_im), (pr, w_im), (pi, w_re))):
                    e.tensor_tensor(prod[q], f, w, ALU.mult).then_inc(sem("remod"), 1)

            def skip(u):
                e.wait_ge(sem("y_ssm"), u + 1)
                e.scalar_tensor_tensor(out=y_ssm[:, u, :], in0=proj[:, 12 + u, :], scalar=vec(v1, V1, "ssm_d", u),
                                       in1=ps[:, 6, 0:S], op0=ALU.mult, op1=ALU.add).then_inc(sem("y_pre"), 1)

            for u in range(4):
                states(u)
                if u < 3:
                    ahead(lo_split_a, e, "w_in", 2 * u + 2)
                    ahead(lo_split_a, e, "w_in", 2 * u + 3)
                skip(u)
            for u in range(4):
                e.wait_ge(sem("hh"), after("hh", "glu", u + 1))
                e.tensor_tensor(h_lo[:, u, :], y_ssm[:, u, :], h_hi[:, u, :].bitcast(F32), ALU.subtract)\
                    .then_inc(sem("h"), 1)
            for c in range(2):
                ahead(lo_split_a, e, "glu", c)
            e.wait_ge(gu_free, GU_BASE["glu"] + 2)
            e.tensor_tensor(y_ssm, y_ssm, proj[:, 12:16, :], ALU.mult).then_inc(sem("glu_ok"), 1)
            e.wait_ge(sem("root"), after("root", "conv", 1))
            e.reciprocal(rstd[:, 0, :], root[:, 0, :]).then_inc(sem("rstd_mix2"), 1)
            e.wait_ge(sem("root"), after("root", "ssm", 1))
            e.reciprocal(rstd[:, 1, :], root[:, 1, :]).then_inc(sem("rstd_mix2"), 1)
            e.wait_ge(sem("rstd_mix2"), 2)
            for k in range(KD):
                src = proj[:, k, :] if k < 4 else y_ssm[:, k - 4, :]
                g = vec(v1, V1, "out_norm_conv", k) if k < 4 else vec(v1, V1, "out_norm_ssm", k - 4)
                e.scalar_tensor_tensor(out=tmp[:, k, :], in0=src, scalar=g, in1=rstd[:, k // 4, :], op0=ALU.mult,
                                       op1=ALU.mult).then_inc(sem("t"), 1)
            h_los("ymix", tmp, KD)

            def add_out(stage, scale=None):
                for c in range(4):
                    bank = (GU_BASE[stage] + c) % 2
                    e.wait_ge(a_used, A_BASE[stage] + c + 1)
                    if scale is None:
                        e.tensor_tensor(x_t[:, 2 * c:2 * c + 2, :], x_t[:, 2 * c:2 * c + 2, :],
                                        ps[:, bank, :].rearrange("p (t n) -> p t n", t=2), ALU.add).then_inc(x_ok, 1)
                    else:
                        for a in range(2):
                            k = 2 * c + a
                            e.scalar_tensor_tensor(out=x_t[:, k, :], in0=ps[:, bank, a * S:(a + 1) * S],
                                                   scalar=scale(k), in1=x_t[:, k, :], op0=ALU.mult, op1=ALU.add)\
                                .then_inc(x_ok, 1)
                    e.wait_ge(x_ok, X_AFTER(stage, c, scale is not None))
                    e.sem_inc(gu_free, 1)
                    ahead(lo_split_a, e, stage, c)

            def X_AFTER(stage, c, twice):
                base = {"w_out": X_AT["mix"], "a_out": X_AT["a"], "b_out": X_AT["b"]}[stage]
                return base + (c + 1) * (2 if twice else 1)

            add_out("w_out", lambda k: mod[:, 5 * KD + k:5 * KD + k + 1])
            norm_scale(2, 7, "ffn2_norm")
            norm("ffn2", lambda k: nscale[:, 2, k:k + 1], lambda k: mod[:, 6 * KD + k:6 * KD + k + 1])
            feed_forward("ffn2", NF)
            e.wait_ge(sem("ghalf1"), 1)
            add_down("ffn2", lambda k: ghalf[:, 1, k:k + 1])
            rstds("final")
            for k in range(KD):
                e.scalar_tensor_tensor(out=x_t[:, k, :], in0=x_t[:, k, :], scalar=vec(v1, V1, "final_norm", k),
                                       in1=rstd[:, 0, :], op0=ALU.mult, op1=ALU.mult).then_inc(x_ok, 1)

            norm("a", lambda k: vec(v1, V1, "a_norm_2", k))
            e.wait_ge(sem("gate_read"), 1)
            for h in range(GH):
                ins = e.tensor_scalar(cum[:, h * S:(h + 1) * S], acc4[:, h * S:(h + 1) * S],
                                      vec(v1, V1, "a_b_gate_2", h), 0.0, ALU.add, ALU.min)
            ins.then_inc(sem("gate_read"), 1)
            e.wait_ge(sem("gate_read"), 2)
            e.wait_ge(sem("gate_ln"), 1)
            mag = area(8192, 1024)
            e.tensor_tensor(cum, cum, mag, ALU.subtract).then_inc(sem("log_a"), 1)
            e.wait_ge(sem("log_a"), 1)
            for h in range(GH):
                part = cum[:, h * S:(h + 1) * S]
                ins = e.tensor_tensor_scan(part, ones[:, 0:1].to_broadcast([P, S]), part, 0.0, ALU.mult, ALU.add)
            ins.then_inc(sem("cum"), 1)
            e.wait_ge(sem("cum"), 1)
            cum_b = cum.rearrange("p (b n) -> p b n", n=GBLK)
            ref = cum_b[:, :, GBLK // 2 - 1]
            e.tensor_tensor(q_dec.rearrange("p (b n) -> p b n", n=GBLK), cum_b, bcast(ref, GBLK), ALU.subtract)\
                .then_inc(sem("q_arg"), 1)
            for c in range(4):
                ahead(lo_split_a, e, "a_qk", c)
            cum_h = cum.rearrange("p (h n) -> p h n", n=S)
            off = 0
            for b in range(NBLK):
                n = GBLK * (b + 1)
                at = b * GBLK + GBLK // 2 - 1
                dst = k_dec[:, off:off + GH * n].rearrange("p (h n) -> p h n", n=n)
                e.tensor_tensor(dst, bcast(cum_h[:, :, at], n), cum_h[:, :, 0:n], ALU.subtract).then_inc(sem("k_arg"), 1)
                off += GH * n
                if b % 2 == 1:
                    ahead(lo_split_a, e, "a_v", b // 2)
            e.wait_ge(sem("q_exp"), 1)
            e.wait_ge(gu_free, GU_BASE["a_qk"] + 4)
            e.scalar_tensor_tensor(out=q_dec, in0=area(0, 1024), scalar=float(GDK) ** -0.5, in1=q_dec, op0=ALU.mult,
                                   op1=ALU.mult).then_inc(sem("qdec"), 1)
            off = 0
            for b in range(NBLK):
                n = GBLK * (b + 1)
                dst = k_dec[:, off:off + GH * n].rearrange("p (h n) -> p h n", n=n)
                e.wait_ge(sem("k_exp"), b + 1)
                e.tensor_tensor(dst, dst, qk[:, 4:8, 0:n], ALU.mult).then_inc(sem("kdec"), 1)
                off += GH * n
            for c in range(4):
                ahead(lo_split_a, e, "a_g", c)
            e.wait_ge(sem("z"), 1)
            e.wait_ge(sem("h"), after("h", "a", KD))
            e.memset(tmp_flat, 0.0).then_inc(sem("at_zero"), 1)
            e.wait_ge(sem("masks"), 5)
            e.wait_ge(sem("att"), 1)
            e.wait_ge(sem("at_zero"), 1)
            at4 = at_sb.rearrange("p (j h n) -> p j h n", j=2, h=GH)
            ap4 = acc4.rearrange("p (j h n) -> p j h n", j=2, h=GH)
            for b in range(NBLK):
                jt, m = b // 4, GBLK * (b % 4 + 1)
                i0 = b * GBLK
                mask = tri[0:m, i0 % P:i0 % P + GBLK].unsqueeze(1).to_broadcast([m, GH, GBLK])
                e.tensor_tensor(at4[0:m, jt, :, i0:i0 + GBLK], ap4[0:m, jt, :, i0:i0 + GBLK], mask, ALU.mult)\
                    .then_inc(sem("at_sb"), 1)
            e.tensor_copy(at4[:, 0, :, P:S], ap4[:, 0, :, P:S]).then_inc(sem("at_sb"), 1)
            e.wait_ge(sem("oroot_a"), 1)
            orstd = k_dec[:, 3072:4096]
            e.reciprocal(orstd, k_dec[:, 2048:3072]).then_inc(sem("orstd_a"), 1)
            e.wait_ge(sem("orstd_a"), 1)
            for t in range(KD):
                e.scalar_tensor_tensor(out=silu_g[:, t, :], in0=silu_g[:, t, :], scalar=vec(v1, V1, "a_head_norm_2", t % 2),
                                       in1=orstd[:, (t // 2) * S:(t // 2 + 1) * S], op0=ALU.mult, op1=ALU.mult)\
                    .then_inc(sem("g_scaled"), 1)
            for t in range(KD):
                e.wait_ge(sem("g_scaled"), t + 1)
                e.tensor_tensor(tmp[:, t, :], acc4[:, t * S:(t + 1) * S], silu_g[:, t, :], ALU.mult)\
                    .then_inc(sem("t"), 1)
            h_los("oa", tmp, KD)
            add_out("a_out")
            norm("mlp0", lambda k: vec(v1, V1, "mlp_norm_2", k))
            feed_forward("mlp0", NHID)
            add_down("mlp0")

            rstds("kv")
            scaled("kv", lambda k: vec(v1, V1, "kv_norm_2", k))
            h_los("kv", tmp, KD)
            for c in range(4):
                ahead(lo_split_a, e, "b_k", c)
            for c in range(4):
                ahead(lo_split_a, e, "b_v", c)
            e.wait_ge(a_used, A_BASE["b_v"] + 4)
            scaled("b", lambda k: vec(v1, V1, "b_norm_2", k))
            h_los("b", tmp, KD)
            for c in range(4):
                ahead(lo_split_a, e, "b_q", c)
            e.wait_ge(sem("ld_att"), 16 * 3)
            for a in range(2):
                e.tensor_tensor(st_lam[:, a, :], lamp[:, 2 * a, :], lamp[:, 2 * a + 1, :], ALU.mult)\
                    .then_inc(sem("lam_prod"), 1)
            e.wait_ge(sem("lam_prod"), 2)
            e.tensor_reduce(lam_s[:, 0:2], st_lam[:, :, :], AX.X, ALU.add).then_inc(sem("lam_dots"), 1)
            e.wait_ge(sem("kroot"), 1)
            e.reciprocal(tmp_flat, tmp_flat).then_inc(sem("krstd"), 1)
            e.wait_ge(sem("krstd"), 1)
            e.scalar_tensor_tensor(out=area(0, 2048), in0=area(0, 2048), scalar=vec(v2, V2, "k_norm_2", 0),
                                   in1=tmp_flat, op0=ALU.mult, op1=ALU.mult).then_inc(sem("k_n"), 1)
            e.wait_ge(sem("qroot"), 1)
            e.reciprocal(area(6144, 2048), area(6144, 2048)).then_inc(sem("qrstd"), 1)
            e.tensor_scalar(qgain[:, :], vec(v2, V2, "b_q_norm_2", 0), float(DD) ** -0.5, None, ALU.mult)\
                .then_inc(sem("qrstd"), 1)
            e.wait_ge(sem("qrstd"), 2)
            e.scalar_tensor_tensor(out=area(4096, 2048), in0=area(4096, 2048), scalar=qgain[:, 0:1],
                                   in1=area(6144, 2048), op0=ALU.mult, op1=ALU.mult).then_inc(sem("q_n"), 1)
            e.wait_ge(sem("q_n"), 1)
            e.wait_ge(sem("lam_exp"), 1)
            e.tensor_tensor(lam_s[:, 4:5], lam_s[:, 3:4], lam_s[:, 2:3], ALU.subtract).then_inc(sem("lam_neg"), 1)
            e.wait_ge(sem("lam_neg"), 1)
            e.tensor_scalar(lam_s[:, 5:6], lam_s[:, 4:5], -LAM_INIT, None, ALU.add).then_inc(sem("lam_neg"), 1)

            def weights(h):
                hb = h % 2
                st = st_s[:, hb, :]
                e.wait_ge(sem("p_exp"), 4 * (h + 1))
                e.reciprocal(st[:, 8:12], st[:, 4:8]).then_inc(sem("p_rec"), 1)
                e.wait_ge(sem("p_rec"), h + 1)
                e.wait_ge(sem("lam_neg"), 2)
                e.tensor_scalar(st[:, 12:16], st[:, 8:12], lam_s[:, 5:6], None, ALU.mult).then_inc(sem("p_lam"), 1)
                e.wait_ge(sem("p_lam"), h + 1)
                if h >= 2:
                    e.wait_ge(sem("a_turned"), h - 1)
                for q in range(2):
                    n, o = (S, P) if q else (P, 0)
                    p0 = p_sb[:, hb * 768 + o:hb * 768 + o + n]
                    p1 = p_sb[:, hb * 768 + 384 + o:hb * 768 + 384 + o + n]
                    e.tensor_scalar(p1, p1, st[:, 13 + 2 * q:14 + 2 * q], None, ALU.mult).then_inc(sem("p1_ok"), 1)
                for q in range(2):
                    n, o = (S, P) if q else (P, 0)
                    p0 = p_sb[:, hb * 768 + o:hb * 768 + o + n]
                    p1 = p_sb[:, hb * 768 + 384 + o:hb * 768 + 384 + o + n]
                    e.wait_ge(sem("p1_ok"), 2 * h + q + 1)
                    e.scalar_tensor_tensor(out=a_sb[:, hb * 384 + o:hb * 384 + o + n], in0=p0,
                                           scalar=st[:, 8 + 2 * q:9 + 2 * q], in1=p1, op0=ALU.mult, op1=ALU.add)\
                        .then_inc(sem("a_ok"), 1)

            def turned(h):
                hb = h % 2
                bank = 0 if hb == 0 else 6
                e.wait_ge(sem("a_turned"), h + 1)
                if h >= 2:
                    e.wait_ge(sem("o_b"), h - 1)
                e.tensor_copy(a_t[:, hb * 384:(hb + 1) * 384], ps[:, bank, 0:384]).then_inc(sem("a_t"), 1)

            def maxima(h):
                hb = h % 2
                bank = 0 if hb == 0 else 6
                e.wait_ge(sem("scores"), h + 1)
                if h >= 2:
                    e.wait_ge(sem("p_exp"), 4 * (h - 1))
                dst = s_sb[:, hb * 768:(hb + 1) * 768].rearrange("p (c n) -> p c n", c=2)
                e.tensor_tensor(dst, ps[:, bank:bank + 2, 0:384],
                                bias_mask[:, :].unsqueeze(1).to_broadcast([P, 2, 384]), ALU.add)\
                    .then_inc(sem("s_read"), 1)
                e.wait_ge(sem("s_read"), h + 1)
                e.tensor_reduce(st_s[:, hb, 0:2], dst[:, :, 0:P], AX.X, ALU.max, negate=True).then_inc(sem("s_max"), 1)
                e.tensor_reduce(st_s[:, hb, 2:4], dst[:, :, P:384], AX.X, ALU.max, negate=True).then_inc(sem("s_max"), 1)

            e.wait_ge(sem("masks"), 5)
            maxima(0)
            for h in range(DH):
                if h + 1 < DH:
                    maxima(h + 1)
                weights(h)
                turned(h)
            for half in range(2):
                e.wait_ge(sem("oroot_b"), half + 1)
                part = area(6144 + half * 1024, 1024)
                e.reciprocal(part, part).then_inc(sem("orstd_b"), 1)
            e.tensor_scalar(qgain[:, :], vec(v1, V1, "b_head_norm_2", 0), 1.0 - LAM_INIT, None, ALU.mult)\
                .then_inc(sem("orstd_b"), 1)
            e.wait_ge(sem("orstd_b"), 3)
            e.wait_ge(sem("oss_b"), 2)
            for t in range(KD):
                e.scalar_tensor_tensor(out=tmp[:, t, :], in0=acc4[:, t * S:(t + 1) * S], scalar=qgain[:, 0:1],
                                       in1=area(6144 + t * S, S), op0=ALU.mult, op1=ALU.mult).then_inc(sem("t"), 1)
            h_los("ob", tmp, KD)
            add_out("b_out")
            norm("mlp1", lambda k: vec(v1, V1, "mlp_norm_2", KD + k))
            feed_forward("mlp1", NHID)
            add_down("mlp1")
            for t in range(2):
                e.wait_ge(sem("x_turned"), 2 * t + 2)
                bank = 7 if t == 0 else 1
                e.tensor_copy(arena[:, t * D + 512:t * D + 1024], ps[:, bank, :]).then_inc(sem("out_rows"), 1)


        @block.gpsimd
        def _(e):
            e.memset(ident[:, :], 0.0).then_inc(sem("id0"), 1)
            e.memset(ones[:, :], 1.0).then_inc(sem("ones"), 1)
            e.wait_ge(sem("id0"), 1)
            e.affine_select(out=ident[:, :], in_=ident[:, :], compare_op=ALU.not_equal, fill=1.0, base=0,
                            pattern=[[-1, P]], channel_multiplier=1).then_inc(sem("ident_ok"), 1)
            for name, n in V1_ROWS:
                at = V1[name][0]
                src = T[name]
                if name == "conv_w":
                    v = src[0].rearrange("w (r c) -> (w r) c", c=P)
                elif name == "mlp_norm_2":
                    v = src.rearrange("l (r c) -> (l r) c", c=P)
                elif name in ("final_norm", "kv_norm_2"):
                    v = src.rearrange("(r c) -> r c", c=P)
                else:
                    v = src[0].rearrange("(r c) -> r c", c=P)
                e.dma_start(v1_rows[at:at + n, :], v).then_inc(sem("ld_v1"), 16)
            for name in ("lambda_re", "lambda_im"):
                at = V2[name][0]
                e.dma_start(v2_rows[at:at + ST, :], T[name][0].rearrange("(t g) n -> t (g n)", g=2))\
                    .then_inc(sem("ld_v2"), 16)
            for name in ("k_norm_2", "b_q_norm_2"):
                at = V2[name][0]
                src = T[name].rearrange("(a n) -> a n", a=1) if name == "k_norm_2" else T[name]
                for c in range(2):
                    e.dma_start(v2_rows[at:at + 1, c * DD:(c + 1) * DD], src).then_inc(sem("ld_v2"), 16)
            for g in range(2):
                e.dma_start(dt_col[g * NST:(g + 1) * NST, :],
                            T["log_dt"][0].rearrange("(t g) -> g t", g=2)[g:g + 1, :].to_broadcast([NST, ST]),
                            allow_slow_non_contiguous=True)\
                    .then_inc(sem("ld_dt"), 16)
            for r, name in enumerate(("ssm_b_re", "ssm_b_im")):
                e.dma_start(b_in[:, r], T[name][0].rearrange("(t g) n c -> (g n) t c", g=2))\
                    .then_inc(sem("ld_b"), 16)
            e.memset(c_in, 0.0).then_inc(sem("c_zero"), 1)
            e.memset(b_bd, 0.0).then_inc(sem("b_zero"), 1)
            e.wait_ge(sem("c_zero"), 1)
            for r, name in enumerate(("ssm_c_re", "ssm_c_im")):
                for a in range(8):
                    e.dma_start(c_in[a * GCH:(a + 1) * GCH, r, :, (a % 2) * NST:(a % 2 + 1) * NST],
                                T[name][0].rearrange("(u a) c n -> a c u n", a=8)[a])\
                        .then_inc(sem("ld_c"), 16)
            e.dma_start(zw[:, :, :], T["a_w_in_2"][0].rearrange("(k p) n -> p k n", p=P)[:, :, 3072:3088])\
                .then_inc(sem("ld_att"), 16)
            e.dma_start(gup[:, :], T["a_w_gate_up_2"][0]).then_inc(sem("ld_att"), 16)
            e.dma_start(lamp[:, :, :].rearrange("p a n -> p (a n)"),
                        T["b_lambda_2"].rearrange("l a n -> l (a n)").to_broadcast([P, 4 * DD]))\
                .then_inc(sem("ld_att"), 16)
            e.memset(ones_blk[:, :], 0.0).then_inc(sem("blk"), 1)
            e.wait_ge(sem("blk"), 1)
            e.memset(ones_blk[0:DD, 0:DD], 1.0).then_inc(sem("masks"), 1)
            e.memset(ones_blk[DD:P, DD:P], 1.0).then_inc(sem("masks"), 1)
            e.wait_ge(sem("masks"), 2)
            e.memset(tri[:, :], 1.0).then_inc(sem("blk"), 1)
            e.memset(bias_mask[:, :], 0.0).then_inc(sem("blk"), 1)
            e.wait_ge(sem("blk"), 3)
            e.affine_select(out=tri[:, :], in_=tri[:, :], compare_op=ALU.is_ge, fill=0.0, base=0,
                            pattern=[[1, P]], channel_multiplier=-1).then_inc(sem("masks"), 1)
            for o in (0, 2 * P):
                e.affine_select(out=bias_mask[:, o:o + P], in_=bias_mask[:, o:o + P], compare_op=ALU.is_ge,
                                fill=MASKED, base=0, pattern=[[-1, P]], channel_multiplier=1)\
                    .then_inc(sem("masks"), 1)
            c = [0]

            def step(ins):
                c[0] += 1
                ins.then_inc(sem("pool_step"), 1)
                e.wait_ge(sem("pool_step"), c[0])

            e.wait_ge(sem("s5_trig"), 2)
            e.wait_ge(sem("t_x"), 1)
            scr = [s5[:, 16 + k, :] for k in range(3)]
            er, ei = s5[:, 14, :], s5[:, 15, :]
            step(e.memset(ph_re[:, :, 0:1], 1.0))
            step(e.memset(ph_im[:, :, 0:1], 0.0))
            step(e.tensor_copy(er, s5[:, 3, :]))
            step(e.tensor_copy(ei, s5[:, 4, :]))
            ta = tiles(area(0, 4096))
            for m in range(8):
                n = 1 << m
                lo_r, lo_i = ph_re[:, :, 0:n], ph_im[:, :, 0:n]
                hi_r, hi_i = ph_re[:, :, n:2 * n], ph_im[:, :, n:2 * n]
                br, bi = bcast(er, n), bcast(ei, n)
                t1, t2 = ta[:, :, 0:n], ta[:, :, P:P + n]
                step(e.tensor_tensor(t1, lo_r, br, ALU.mult))
                step(e.tensor_tensor(t2, lo_i, bi, ALU.mult))
                step(e.tensor_tensor(hi_r, t1, t2, ALU.subtract))
                step(e.tensor_tensor(t1, lo_r, bi, ALU.mult))
                step(e.tensor_tensor(t2, lo_i, br, ALU.mult))
                step(e.tensor_tensor(hi_i, t1, t2, ALU.add))
                if m < 7:
                    step(e.tensor_tensor(scr[0], er, er, ALU.mult))
                    step(e.tensor_tensor(scr[1], ei, ei, ALU.mult))
                    step(e.tensor_tensor(scr[2], er, ei, ALU.mult))
                    step(e.tensor_tensor(er, scr[0], scr[1], ALU.subtract))
                    step(e.tensor_tensor(ei, scr[2], scr[2], ALU.add))
            e.wait_ge(sem("s5_quot"), 1)
            e.wait_ge(sem("ld_b"), 32)
            e.wait_ge(sem("b_zero"), 1)
            qr, qi = bcast(s5[:, 8, :], GCH), bcast(s5[:, 9, :], GCH)
            tb = area(0, 4 * ST * GCH).rearrange("p (q t c) -> p q t c", q=4, c=GCH)
            step(e.tensor_tensor(tb[:, 0], b_in[:, 0], qr, ALU.mult))
            step(e.tensor_tensor(tb[:, 1], b_in[:, 1], qi, ALU.mult))
            step(e.tensor_tensor(tb[:, 2], b_in[:, 0], qi, ALU.mult))
            step(e.tensor_tensor(tb[:, 3], b_in[:, 1], qr, ALU.mult))
            for g in range(2):
                rows, cols = slice(g * NST, (g + 1) * NST), slice(g * GCH, (g + 1) * GCH)
                step(e.tensor_tensor(b_bd[rows, 0, :, cols], tb[rows, 0], tb[rows, 1], ALU.subtract))
                ins = e.tensor_tensor(b_bd[rows, 1, :, cols], tb[rows, 2], tb[rows, 3], ALU.add)
                if g == 0:
                    step(ins)
                else:
                    ins.then_inc(sem("b_bd_ok"), 1)
            e.wait_ge(sem("b_bd_ok"), 1)
            e.wait_ge(gu_free, GU_BASE["w_in"] + 8)
            z = proj[:, 4:8, :]
            w = [bcast(vec(v1, V1, "conv_w", 4 * k, 4), S) for k in range(3)]
            t1 = proj[:, 8:12, :]
            acc = conv_sum[:, :, :]
            cs = sem("conv_ok")
            e.tensor_tensor(z, z, t1, ALU.mult).then_inc(cs, 1)
            e.wait_ge(cs, 1)
            e.tensor_tensor(acc, z, w[2], ALU.mult).then_inc(cs, 1)
            e.tensor_tensor(t1, z, w[1], ALU.mult).then_inc(cs, 1)
            e.wait_ge(cs, 3)
            e.tensor_tensor(acc[:, :, 1:S], acc[:, :, 1:S], t1[:, :, 0:S - 1], ALU.add).then_inc(cs, 1)
            e.wait_ge(cs, 4)
            e.tensor_tensor(t1, z, w[0], ALU.mult).then_inc(cs, 1)
            e.wait_ge(cs, 5)
            e.tensor_tensor(acc[:, :, 2:S], acc[:, :, 2:S], t1[:, :, 0:S - 2], ALU.add).then_inc(cs, 1)
            e.wait_ge(cs, 6)
            e.tensor_tensor(proj[:, 0:4, :], proj[:, 0:4, :], acc, ALU.mult).then_inc(cs, 1)



_INS = [
    "x", "cond", "w_mod", "b_mod", "ffn1_norm", "ffn1_w_gate", "ffn1_w_up", "ffn1_w_down", "mix_norm", "w_in",
    "conv_w", "lambda_re", "lambda_im", "log_dt", "ssm_b_re", "ssm_b_im", "ssm_c_re", "ssm_c_im", "ssm_d", "glu_w",
    "glu_b", "out_norm_conv", "out_norm_ssm", "w_out", "ffn2_norm", "ffn2_w_gate", "ffn2_w_up", "ffn2_w_down",
    "final_norm", "a_norm_2", "a_w_in_2", "a_w_gate_up_2", "a_b_gate_2", "a_head_norm_2", "a_w_out_2",
    "kv_norm_2", "w_kv_2", "k_norm_2", "b_norm_2", "b_w_q_2", "b_q_norm_2", "b_lambda_2", "b_head_norm_2",
    "b_w_out_2", "mlp_norm_2", "mlp_w1_2", "mlp_w2_2",
]


def kernel(**inputs):
    import concourse.bacc as bacc
    import numpy as np
    from concourse.bass_utils import run_bass_kernel_spmd

    nc = bacc.Bacc("TRN2", target_bir_lowering=False, num_devices=1)
    arrays, tensors = {}, {}
    for name in _INS:
        a = np.ascontiguousarray(inputs[name])
        arrays[f"in_{name}"] = a
        tensors[name] = nc.dram_tensor(f"in_{name}", a.shape, mybir.dt.from_np(a.dtype), kind="ExternalInput").ap()
    out = nc.dram_tensor("out_0", (1, S, D), F32, kind="ExternalOutput").ap()
    build(nc, tensors, out)
    r = run_bass_kernel_spmd(nc, [arrays], core_ids=[0])
    return r.results[0]["out_0"]
```

```python
import math
from contextlib import ExitStack

import concourse.bass as bass
from concourse import mybir

F32 = mybir.dt.float32
F32R = mybir.dt.float32r
BF16 = mybir.dt.bfloat16
ACT = mybir.ActivationFunctionType
ALU = mybir.AluOpType
AX = mybir.AxisListType

P = 128
S = 256
D = 1024
KD = D // P
FF = 2816
NF = FF // P
HID = 4096
NHID = HID // P
EPS = 1e-6
N_MOD = 9
MODC = 256
NMODC = N_MOD * D // MODC
MOD0 = 2 * D // MODC
MOD_FFN2 = {0: 32, NF - 3: 33, NF - 2: 34, NF - 1: 35}
MOD_WIDE = 4
GRP, GCH, NST = 32, 16, 64
ST = GRP * NST // P
GH, GDK, GDV = 4, 128, 256
GBLK = 32
NBLK = S // GBLK
KTOT = sum(GBLK * (b + 1) for b in range(NBLK))
TAU = 16.0
DH = 8
DD = 64
LAM_INIT = 0.8 - 0.6 * math.exp(-0.3)
MASKED = -1e30
ROUND = 1.5 * 2 ** 23

A_STAGES = [
    ("ffn1", NF, 2048, 1), ("w_in", 8, 2048, 1), ("glu", 2, 1024, 1), ("w_out", 4, 2048, 1),
    ("ffn2", NF, 2048, 1),
    ("a_qk", 4, 2048, 1), ("a_v", 4, 2048, 0), ("a_g", 4, 2048, 1), ("a_out", 4, 2048, 1),
    ("mlp0", NHID, 1024, 1),
    ("b_k", 4, 2048, 1), ("b_v", 4, 2048, 0), ("b_q", 4, 2048, 1), ("b_out", 4, 2048, 1),
    ("mlp1", NHID, 1024, 1),
]
NEXT = {a[0]: b[0] for a, b in zip(A_STAGES, A_STAGES[1:])}
A_BASE, GU_BASE, A_LEN, A_SIZE = {}, {}, {}, {}
_a = _g = 0
for _name, _n, _size, _gu in A_STAGES:
    A_BASE[_name], GU_BASE[_name], A_LEN[_name], A_SIZE[_name] = _a, _g, _n, _size
    _a += _n
    _g += _n * _gu
D_STAGES = [("ffn1", NF), ("ffn2", NF), ("mlp0", NHID), ("mlp1", NHID)]
D_BASE, _d = {}, 0
for _name, _n in D_STAGES:
    D_BASE[_name] = _d
    _d += _n
D_TOTAL = _d
A_ORDER = [(s, c) for s, n, _, _ in A_STAGES for c in range(n)]
WIN_TILES = [12, 13, 14, 15, 4, 5, 8, 9, 6, 7, 10, 11, 0, 1, 2, 3]
NORMS = ["ffn1", "mix", "ffn2", "final", "a", "mlp0", "kv", "b", "mlp1"]

V0 = {"b_mod": (0, 72), "cond": (72, 8)}
V1_ROWS = [("ffn1_norm", 8), ("mix_norm", 8), ("ffn2_norm", 8), ("final_norm", 8), ("a_norm_2", 8),
           ("kv_norm_2", 8), ("b_norm_2", 8), ("mlp_norm_2", 16), ("out_norm_conv", 4),
           ("out_norm_ssm", 4), ("ssm_d", 4), ("glu_b", 4), ("a_b_gate_2", 4), ("conv_w", 12),
           ("a_head_norm_2", 2), ("b_head_norm_2", 1)]
V2_ROWS = [("lambda_re", 16), ("lambda_im", 16), ("k_norm_2", 1), ("b_q_norm_2", 1)]


def columns(rows):
    at, out = 0, {}
    for name, n in rows:
        out[name] = (at, n)
        at += n
    return out, at


V1, V1_N = columns(V1_ROWS)
V2, V2_N = columns(V2_ROWS)


ORDER = ["ffn1", "mix", "glu", "conv", "ssm", "ymix", "ffn2", "final", "a", "oa", "mlp0", "kv", "b", "ob", "mlp1"]
COUNTS = {
    "sq": {"conv": 2, "ssm": 2, "glu": 0, "ymix": 0, "oa": 0, "b": 0, "ob": 0},
    "ss": {"glu": 0, "ymix": 0, "oa": 0, "b": 0, "ob": 0},
    "t": {"glu": 0, "conv": 0, "ssm": 0, "final": 0, "a": 0, "mlp0": 0, "kv": 0, "b": 0, "mlp1": 0},
    "hh": {"glu": 4, "conv": 0, "ssm": 0, "final": 0},
}
EACH = {"sq": 4, "ss": 1, "root": 1, "rtok": 1, "rb": 1, "t": KD, "hh": KD, "h": KD}
for _k in ("root", "rtok", "rb"):
    COUNTS[_k] = COUNTS["ss"]
COUNTS["h"] = COUNTS["hh"]
LATE = ["a", "mlp0", "kv", "mlp1"]


def after(kind, name, v):
    return v + sum(COUNTS[kind].get(n, EACH[kind]) for n in ORDER[:ORDER.index(name)])


def lin(v, i, m):
    return v if i is None else i * m + v


def build(nc, T, out):
    ctx = ExitStack()
    with ctx:
        def sb(name, shape, dt=F32):
            return ctx.enter_context(nc.sbuf_tensor(name, shape, dt))

        sems = {}

        def sem(name):
            if name not in sems:
                sems[name] = ctx.enter_context(nc.semaphore(name))
            return sems[name]

        x_t = sb("x_t", [P, KD, S])
        h_hi = sb("h_hi", [P, KD, S], F32R)
        h_lo = sb("h_lo", [P, KD, S], F32R)
        tmp = sb("tmp", [P, KD, S])
        raw_a = sb("raw_a", [P, 2, 2048])
        hi_a = sb("hi_a", [P, 2, 2048], F32R)
        lo_a = sb("lo_a", [P, 2, 2048], F32R)
        raw_d = sb("raw_d", [P, 2, D])
        hi_d = sb("hi_d", [P, 2, D], F32R)
        lo_d = sb("lo_d", [P, 2, D], F32R)
        raw_m = sb("raw_m", [P, 2, KD, MODC])
        acc_m = sb("acc_m", [P, 2, MODC])
        gate = sb("gate", [P, 2, S])
        hid = sb("hid", [P, 2, S])
        hid_hi = sb("hid_hi", [P, 2, S], F32R)
        hid_lo = sb("hid_lo", [P, 2, S], F32R)
        root_t = sb("root_t", [P, 2, 2])
        r_tok = sb("r_tok", [P, 2, 2])
        rs = sb("rs", [P, S])
        ident = sb("ident", [P, P])
        ones = sb("ones", [P, P])
        eps = sb("eps", [P, 1])
        v0_rows, v1_rows, v2_rows = gate[0:80, 0, 0:P], gate[0:V1_N, 0, P:S], gate[0:V2_N, 1, 0:P]
        v0 = sb("v0", [P, 80])
        v1 = sb("v1", [P, V1_N])
        v2 = sb("v2", [P, V2_N])
        cact = sb("cact", [P, KD])
        mod = sb("mod", [P, N_MOD * KD])
        nscale = sb("nscale", [P, 3, KD])
        ghalf = sb("ghalf", [P, 2, KD])
        arena = sb("arena", [P, 13312])
        ps = ctx.enter_context(nc.psum_tensor("ps", [P, 8, 512], F32))
        def acc_tile(t):
            return ps[:, 2 + t // 2, (t % 2) * S:(t % 2 + 1) * S]

        psf = ps[:, :, :].rearrange("p b n -> p (b n)")
        acc4 = psf[:, 1024:3072]

        def area(at, n):
            return arena[:, at:at + n]

        def tiles(ap, n=S):
            return ap.rearrange("p (t n) -> p t n", n=n)

        raw_m_flat = raw_m[:, :, :, :].rearrange("p a k n -> p (a k n)")
        tmp_flat = tmp[:, :, :].rearrange("p k n -> p (k n)")

        proj = tiles(area(0, 4096))
        ph_re, ph_im = tiles(area(4096, 4096)), tiles(area(8192, 4096))
        y_ssm = tiles(area(12288, 1024))
        w_re, w_im = tmp_flat[:, 0:1024], tmp_flat[:, 1024:2048]
        prod = [raw_m_flat[:, 1024 * k:1024 * (k + 1)] for k in range(4)]
        conv_sum = sb("conv_sum", [P, 4, S])
        dt_col = sb("dt_col", [P, ST])
        s5 = sb("s5", [P, 19, ST])
        b_bd = conv_sum[:, :, :].rearrange("p t n -> p (t n)").rearrange("p (r t c) -> p r t c", r=2, c=2 * GCH)
        b_t = sb("b_t", [P, 2, 4, P])
        c_in = area(12288, 1024).rearrange("p (r u n) -> p r u n", r=2, u=4)
        c_t = sb("c_t", [P, 3, 4, P])
        b_in = c_t[:, 0].rearrange("p u n -> p (u n)").rearrange("p (r t c) -> p r t c", r=2, c=GCH)
        zw = sb("zw", [P, KD, 16])
        gup = sb("gup", [16, GH * GDK])
        z_sb = sb("z_sb", [16, S])
        tri = sb("tri", [P, P])
        mask_b = sb("mask_b", [P, P], BF16)
        ident_b = sb("ident_b", [P, P], BF16)
        lamp = sb("lamp", [P, 4, DD])
        lam_s = sb("lam_s", [P, 8])

        qk = tiles(area(0, 2048))
        v_rows = area(2048, 2048).rearrange("p (t n) -> p t n", t=2)
        silu_g = tiles(area(4096, 2048))
        cum = area(6144, 1024)
        q_dec = area(7168, 1024)
        k_dec = area(8192, GH * KTOT)
        at_sb = tmp_flat
        k_n = tiles(area(0, 2048))
        q_n = tiles(area(4096, 2048))
        zero_w = sb("zero_w", [P, P], F32R)
        p_sb = area(7680, 2 * 768)
        o_b = tiles(area(10752, 2048))
        a_sb = area(9216, 2 * 384)
        a_t = area(9984, 2 * 384)
        st_lam = sb("st_lam", [P, 2, DD])
        qgain = sb("qgain", [P, 1])
        st_s = sb("st_s", [P, 2, 32])
        ones_2 = sb("ones_2", [P, 2])
        k_r, q_r = sb("k_r", [P, 32]), sb("q_r", [P, 32])

        gate_flat = gate[:, :, :].rearrange("p t n -> p (t n)")

        def vec(tile, table, name, k, n=1):
            at = table[name][0]
            return tile[:, at + k:at + k + n]

        def bcast(ap, n):
            return ap.unsqueeze(2).to_broadcast([ap.shape[0], ap.shape[1], n])

        def kt(w, k=KD):
            return w.rearrange("(k p) n -> p k n", p=P)

        wv = {
            "g1": kt(T["ffn1_w_gate"][0]), "u1": kt(T["ffn1_w_up"][0]),
            "g2": kt(T["ffn2_w_gate"][0]), "u2": kt(T["ffn2_w_up"][0]),
            "w_in": kt(T["w_in"][0]), "glu": kt(T["glu_w"][0]), "w_out": kt(T["w_out"][0]),
            "a_in": kt(T["a_w_in_2"][0]), "a_out": kt(T["a_w_out_2"][0]),
            "kv": kt(T["w_kv_2"]), "b_q": kt(T["b_w_q_2"][0]), "b_out": kt(T["b_w_out_2"][0]),
            "mlp0": kt(T["mlp_w1_2"][0]), "mlp1": kt(T["mlp_w1_2"][1]),
            "mod": kt(T["w_mod"][0]),
        }
        dv = {"ffn1": kt(T["ffn1_w_down"][0]), "ffn2": kt(T["ffn2_w_down"][0]),
              "mlp0": kt(T["mlp_w2_2"][0]), "mlp1": kt(T["mlp_w2_2"][1])}

        a_loaded = [sem("a_loaded0"), sem("a_loaded1")]
        d_loaded = [sem("d_loaded0"), sem("d_loaded1")]
        m_loaded = [sem("m_loaded0"), sem("m_loaded1")]
        a_hi, a_split, a_used = sem("a_hi"), sem("a_split"), sem("a_used")
        d_hi, d_split, d_used = sem("d_hi"), sem("d_split"), sem("d_used")
        m_summed, m_step = sem("m_summed"), sem("m_step")
        gu_free = sem("gu_free")
        gated, hid_hi_ok, hid_ok = sem("gated"), sem("hid_hi_ok"), sem("hid_ok")
        x_ok = sem("x_ok")
        block = ctx.enter_context(nc.Block())

        X_AT, n = {}, 2
        for name in NORMS:
            X_AT[name] = n
            n += {"ffn1": 8, "mix": 8, "ffn2": 8, "final": 8, "a": 4, "mlp0": 8, "kv": 0, "b": 4,
                  "mlp1": 8}[name]
        X_FROM = {"mix": (8, 1), "ffn2": (8, 1), "final": (8, 1), "a": (8, 1), "mlp0": (4, 2), "kv": (8, 1),
                  "mlp1": (4, 2)}

        def load_a(e, stage, c, i=None):
            ca = A_BASE[stage] + c
            slot = ca % 2
            if i is not None or ca >= 2:
                e.wait_ge(a_split, lin(ca - 1, i, 2))
            lo, hi = raw_a[:, slot, 0:1024], raw_a[:, slot, 1024:2048]
            if stage in ("ffn1", "ffn2"):
                n = stage[-1]
                cols = bass.ds(lin(c * P, i, 2 * P), P)
                parts = [(lo.rearrange("p (k n) -> p k n", k=KD), wv["g" + n][:, :, cols]),
                         (hi.rearrange("p (k n) -> p k n", k=KD), wv["u" + n][:, :, cols])]
            elif stage in ("mlp0", "mlp1"):
                cols = bass.ds(lin(c * P, i, 2 * P), P)
                t = lo.rearrange("p (k n) -> p k n", k=KD)
                parts = [(t[:, 0:4, :], wv[stage][:, 0:4, cols]), (t[:, 4:8, :], wv[stage][:, 4:8, cols])]
            elif stage == "glu":
                t = lo.rearrange("p (a k n) -> p a k n", a=2, k=4)
                parts = [(t[:, a], wv["glu"][:, :, (2 * c + a) * P:(2 * c + a + 1) * P]) for a in range(2)]
            elif stage in ("a_v", "b_v"):
                w = wv["a_in"] if stage == "a_v" else wv["kv"]
                parts = [(h, w[:, 2 * c + a, 1024:2048]) for a, h in enumerate((lo, hi))]
            else:
                w, cols = {
                    "w_in": (wv["w_in"], [P * t for t in WIN_TILES]),
                    "w_out": (wv["w_out"], [P * t for t in range(8)]),
                    "a_qk": (wv["a_in"], [P * t for t in range(8)]),
                    "a_g": (wv["a_in"], [2048 + P * t for t in range(8)]),
                    "a_out": (wv["a_out"], [P * t for t in range(8)]),
                    "b_k": (wv["kv"], [P * t for t in range(8)]),
                    "b_q": (wv["b_q"], [P * t for t in range(8)]),
                    "b_out": (wv["b_out"], [P * t for t in range(8)]),
                }[stage]
                parts = [(h.rearrange("p (k n) -> p k n", k=KD), w[:, :, cols[2 * c + a]:cols[2 * c + a] + P])
                         for a, h in enumerate((lo, hi))]
            for dst, src in parts:
                e.dma_start(dst, src).then_inc(a_loaded[slot], 16)

        def load_a_ahead(e, stage, c):
            at = A_BASE[stage] + c + 4
            if at < len(A_ORDER):
                load_a(e, *A_ORDER[at])

        def load_d(e, d, i=None):
            if i is None and d >= D_TOTAL:
                return
            stage = [s for s, _ in D_STAGES if D_BASE[s] <= d][-1]
            slot = d % 2
            if i is not None or d >= 2:
                e.wait_ge(d_split, lin(d - 1, i, 2))
            e.dma_start(raw_d[:, slot, :].unsqueeze(1),
                        dv[stage][:, bass.ds(lin(d - D_BASE[stage], i, 2), 1), :])\
                .then_inc(d_loaded[slot], 16)

        def mod_slot(m):
            if m < MOD_WIDE:
                return area(4096 + m * KD * MODC, KD * MODC).rearrange("p (k n) -> p k n", k=KD)
            return raw_m[:, m % 2, :, :]

        def load_m(e, m, i=None):
            if m < MOD_WIDE:
                e.dma_start(mod_slot(m), wv["mod"][:, :, m * MODC:(m + 1) * MODC]).then_inc(sem(f"m_first{m}"), 16)
                return
            if i is not None or m >= MOD_WIDE + 2:
                e.wait_ge(m_summed, lin(m - 1, i, 2))
            e.dma_start(mod_slot(m), wv["mod"][:, :, bass.ds(lin(m * MODC, i, 2 * MODC), MODC)])\
                .then_inc(m_loaded[m % 2], 16)

        @block.sync
        def _(e):
            for m in range(MOD_WIDE + 2):
                load_m(e, m)
            load_a(e, "ffn1", 0)
            load_a(e, "ffn1", 1)
            load_m(e, MOD_WIDE + 2)
            load_d(e, 0)
            load_m(e, MOD_WIDE + 3)
            load_d(e, 1)
            load_a(e, "ffn1", 2)
            load_a(e, "ffn1", 3)
            load_m(e, MOD0)
            load_m(e, MOD0 + 1)
            load_m(e, MOD0 + 2)
            load_d(e, 2)

            def feed_forward_loads(stage, n):
                with_mod = stage == "ffn1"
                db = D_BASE[stage]
                with e.Fori(0, (n - 4) // 2) as i:
                    for s in range(2):
                        load_a(e, stage, s + 4, i)
                        load_d(e, db + s + 3, i)
                        if with_mod:
                            load_m(e, MOD0 + 3 + s, i)
                for f in range(n - 4, n):
                    load_a_ahead(e, stage, f)
                    load_d(e, db + f + 3)
                    if with_mod:
                        if f < n - 1:
                            load_m(e, MOD0 + 3 + f)
                    if stage == "ffn2" and f in (n - 4, n - 3):
                        load_m(e, 34 + f - (n - 4))

            for stage, n, _, _ in A_STAGES:
                if stage in D_BASE:
                    feed_forward_loads(stage, n)
                else:
                    for c in range(n):
                        load_a_ahead(e, stage, c)
                        if stage == "w_out" and c == 0:
                            e.wait_ge(sem("y_ssm"), 4)
                            load_m(e, 32)
                            load_m(e, 33)
            e.wait_ge(sem("out_rows"), 4)
            for t in range(2):
                e.dma_start(out[0, t * P:(t + 1) * P, :],
                            arena[:, t * D:(t + 1) * D]).then_inc(sem("stored"), 16)
            e.wait_ge(sem("stored"), 32)

        def hi_split_a(e, ca, i=None, size=None):
            slot = ca % 2
            size = size or A_SIZE[A_ORDER[ca][0]]
            e.wait_ge(a_loaded[slot], lin(32 * (ca // 2 + 1), i, 32))
            if i is not None or ca >= 2:
                e.wait_ge(a_used, lin(ca - 1, i, 2))
            e.activation(hi_a[:, slot, 0:size], raw_a[:, slot, 0:size], ACT.Copy).then_inc(a_hi, 1)

        def lo_split_a(e, ca, i=None, size=None):
            slot = ca % 2
            size = size or A_SIZE[A_ORDER[ca][0]]
            e.wait_ge(a_hi, lin(ca + 1, i, 2))
            e.tensor_tensor(lo_a[:, slot, 0:size], raw_a[:, slot, 0:size],
                            hi_a[:, slot, 0:size].bitcast(F32), ALU.subtract).then_inc(a_split, 1)

        def hi_split_d(e, d, i=None):
            if i is None and d >= D_TOTAL:
                return
            slot = d % 2
            e.wait_ge(d_loaded[slot], lin(16 * (d // 2 + 1), i, 16))
            if i is not None or d >= 2:
                e.wait_ge(d_used, lin(d - 1, i, 2))
            e.activation(hi_d[:, slot, :], raw_d[:, slot, :], ACT.Copy).then_inc(d_hi, 1)

        def lo_split_d(e, d, i=None):
            if i is None and d >= D_TOTAL:
                return
            slot = d % 2
            e.wait_ge(d_hi, lin(d + 1, i, 2))
            e.tensor_tensor(lo_d[:, slot, :], raw_d[:, slot, :],
                            hi_d[:, slot, :].bitcast(F32), ALU.subtract).then_inc(d_split, 1)

        def ahead(split, e, stage, c):
            at = A_BASE[stage] + c + 2
            if at < len(A_ORDER):
                split(e, at)

        def feed_forward_steps(e, n, step):
            step(0, None)
            with e.Fori(0, (n - 4) // 2) as i:
                for s in range(2):
                    step(1 + s, i)
            for f in range(n - 3, n):
                step(f, None)

        def three(e, dst, w_hi, w_lo, r_hi, r_lo, start, stop):
            e.matmul(dst, w_hi, r_hi, start=start, stop=False, skip_group_check=True)
            e.matmul(dst, w_hi, r_lo, start=False, stop=False, skip_group_check=True)
            return e.matmul(dst, w_lo, r_hi, start=False, stop=stop, skip_group_check=True)

        @block.tensor
        def _(e):
            def in_tile(slot, t, dst, kn, first=None):
                for k in range(kn):
                    at = t * kn * P + k * P
                    if first:
                        e.wait_ge(sem("h"), after("h", first, k + 1))
                    mm = three(e, dst, hi_a[:, slot, at:at + P], lo_a[:, slot, at:at + P],
                               h_hi[:, k, :], h_lo[:, k, :], k == 0, k == kn - 1)
                return mm

            def gu_chunk(stage, f, i=None, nt=2, kn=KD, first=None):
                ca, g = A_BASE[stage] + f, GU_BASE[stage] + f
                slot, bank = ca % 2, g % 2
                e.wait_ge(a_split, lin(ca + 1, i, 2))
                if i is not None or g >= 2:
                    e.wait_ge(gu_free, lin(g - 1, i, 2))
                for t in range(nt):
                    mm = in_tile(slot, t, ps[:, bank, t * S:(t + 1) * S], kn, first if t == 0 else None)
                mm.then_inc(a_used, 1)

            def down(stage, f, i=None, last=False):
                d = D_BASE[stage] + f
                slot = d % 2
                e.wait_ge(d_split, lin(d + 1, i, 2))
                e.wait_ge(hid_ok, lin(d + 1, i, 2))
                for t in range(KD):
                    mm = three(e, acc_tile(t),
                               hi_d[:, slot, t * P:(t + 1) * P], lo_d[:, slot, t * P:(t + 1) * P],
                               hid_hi[:, slot, :], hid_lo[:, slot, :], False, last)
                    if last and t in (1, 3, 5):
                        mm.then_inc(sem("acc_ok"), 1)
                mm.then_inc(d_used, 1)

            def mod_sum(m, i=None):
                e.wait_ge(m_summed, lin(m + 1, i, 2))
                for t in range(2):
                    mm = e.matmul(ps[:, 7, bass.ds(lin(2 * m + t, i, 4), 1)], acc_m[:, m % 2, t * P:(t + 1) * P],
                                  ones[:, 0:1], start=True, stop=True)
                mm.then_inc(sem("m_done"), 1)

            def feed_forward(stage, n, nt):
                with_mod = stage == "ffn1"
                gu_chunk(stage, 0, None, nt, first=stage)
                clear_acc()
                if stage in LATE:
                    sum_squares(stage, KD)
                    on_partitions(stage)
                if with_mod:
                    mod_sum(MOD0)
                with e.Fori(0, (n - 2) // 2) as i:
                    for s in range(2):
                        gu_chunk(stage, 1 + s, i, nt)
                        if with_mod:
                            mod_sum(MOD0 + 1 + s, i)
                        down(stage, s, i)
                if stage == "ffn2":
                    mod_sum(32)
                gu_chunk(stage, n - 1, None, nt)
                if with_mod:
                    mod_sum(MOD0 + n - 1)
                if stage == "ffn2":
                    mod_sum(33)
                down(stage, n - 2)
                if stage == "ffn2":
                    mod_sum(34)
                down(stage, n - 1, None, True)
                if stage == "ffn2":
                    mod_sum(35)

            def clear_acc():
                e.wait_ge(sem("zero_ok"), 1)
                for b in range(4):
                    e.matmul(ps[:, 2 + b, :], zero_w[:, :], h_hi[:, 0:2, :], start=True, stop=False,
                             skip_group_check=True)

            def sum_squares(name, n, bank=6, src=None):
                src = tmp if src is None else src
                for t in range(2):
                    for k in range(n):
                        if t == 0 and k % 2 == 0:
                            e.wait_ge(sem("sq"), after("sq", name, k // 2 + 1))
                        mm = e.matmul(ps[:, bank, t:t + 1], src[:, k, t * P:(t + 1) * P], ones[:, 0:1],
                                      start=(k == 0), stop=(k == n - 1))
                mm.then_inc(sem("ss"), 1)

            def on_partitions(name, bank=6, slot=0):
                e.wait_ge(sem("rtok"), after("rtok", name, 1))
                for t in range(2):
                    mm = e.matmul(ps[:, bank, S + t * P:S + (t + 1) * P], r_tok[:, slot, t:t + 1].to_broadcast([P, P]),
                                  ident[:, :], start=True, stop=True, skip_group_check=True)
                mm.then_inc(sem("rb"), 1)

            def project(stage, n, first, nt=2, kn=KD):
                for c in range(n):
                    gu_chunk(stage, c, None, nt, kn, first if c == 0 else None)

            def rows_product(stage):
                for c in range(4):
                    ca = A_BASE[stage] + c
                    slot = ca % 2
                    e.wait_ge(a_split, ca + 1)
                    for a in range(2):
                        k = 2 * c + a
                        for t in range(2):
                            hh, hl = h_hi[:, k, t * P:(t + 1) * P], h_lo[:, k, t * P:(t + 1) * P]
                            for half in range(2):
                                at = a * 1024 + half * 512
                                w_hi, w_lo = hi_a[:, slot, at:at + 512], lo_a[:, slot, at:at + 512]
                                dst = ps[:, 2 + 2 * t + half, :]
                                e.matmul(dst, hh, w_hi, start=(k == 0), stop=False, skip_group_check=True)
                                e.matmul(dst, hh, w_lo, start=False, stop=False, skip_group_check=True)
                                mm = e.matmul(dst, hl, w_hi, start=False, stop=(k == 7), skip_group_check=True)
                    mm.then_inc(a_used, 1)

            e.wait_ge(sem("ident_ok"), 1)
            e.wait_ge(sem("ones"), 1)
            e.wait_ge(sem("ld_v0"), 32)
            e.transpose(ps[:, 6, 0:80], v0_rows, ident[0:80, 0:80]).then_inc(sem("t_v0"), 1)
            e.wait_ge(sem("ld_x"), 16)
            for k in range(KD):
                for t in range(2):
                    mm = e.transpose(ps[:, 2 + k // 2, (k % 2) * S + t * P:(k % 2) * S + (t + 1) * P],
                                     arena[:, t * D + k * P:t * D + (k + 1) * P], ident[:, :])
            mm.then_inc(sem("t_x"), 1)
            e.wait_ge(sem("v0_ok"), 1)
            sum_squares("ffn1", KD)
            on_partitions("ffn1")
            for m in range(MOD0):
                mod_sum(m)
                if m == 3:
                    e.wait_ge(sem("ld_v1"), 16 * len(V1_ROWS))
                    e.transpose(ps[:, 0, 0:V1_N], v1_rows, ident[0:V1_N, 0:V1_N]).then_inc(sem("t_v1"), 1)
                    e.wait_ge(sem("ld_v2"), 16 * 6)
                    e.transpose(ps[:, 1, 0:V2_N], v2_rows, ident[0:V2_N, 0:V2_N]).then_inc(sem("t_v2"), 1)
            e.wait_ge(x_ok, 2)
            e.wait_ge(sem("v12_ok"), 2)
            feed_forward("ffn1", NF, 2)

            e.wait_ge(sem("b_bd_ok"), 1)
            e.wait_ge(sem("ld_c"), 16 * 16)
            for q, (src, bank) in enumerate(((b_bd, 6), (b_bd, 0), (c_in, 1), (c_in, 6))):
                if q == 3:
                    e.wait_ge(sem("bc_t_ok"), 1)
                for u in range(4):
                    if q < 2:
                        part = b_bd[:, q, 4 * u:4 * u + 4, :].rearrange("p t c -> p (t c)")
                    else:
                        part = c_in[:, q - 2, u, :]
                    mm = e.transpose(ps[:, bank, u * P:(u + 1) * P], part, ident[:, :])
                mm.then_inc(sem("bc_t"), 1)
            e.wait_ge(sem("bc_t_ok"), 5)
            sum_squares("mix", KD)
            on_partitions("mix")

            def ssm_inputs(u):
                if u >= 1:
                    e.wait_ge(sem("bu_read"), u)
                for half in range(2):
                    if half == 1:
                        e.wait_ge(sem("bu_half"), u + 1)
                    for r in range(2):
                        for j in (half, half + 2):
                            rows = slice(32 * j, 32 * j + 32)
                            mm = e.matmul(ps[:, 2 + 2 * r + j // 2, (j % 2) * S:(j % 2 + 1) * S],
                                          b_t[rows, r, u, :], proj[rows, 12 + u, :], start=True, stop=True,
                                          skip_group_check=True)
                    mm.then_inc(sem("bu" if half else "bu_half"), 1)

            def ssm_outputs(u):
                e.wait_ge(sem("remod"), 4 * (u + 1))
                if u >= 1:
                    e.wait_ge(sem("y_pre"), u)
                for j in range(4):
                    rows = slice(32 * j, 32 * j + 32)
                    for q, which in enumerate((0, 1, 2, 2)):
                        mm = e.matmul(ps[rows, 6, 0:S], c_t[:, which, u, rows], prod[q][:, j * S:(j + 1) * S],
                                      start=(q == 0), stop=(q == 3), skip_group_check=True)
                mm.then_inc(sem("y_ssm"), 1)

            for c in range(8):
                gu_chunk("w_in", c, first="mix" if c == 0 else None)
                if c == 0:
                    mod_sum(30)
                    mod_sum(31)
                if c % 2 == 1:
                    u = c // 2
                    e.wait_ge(gu_free, GU_BASE["w_in"] + 2)
                    ssm_inputs(u)
                    if u >= 1:
                        ssm_outputs(u - 1)
            ssm_outputs(3)
            sum_squares("conv", 4, 2)
            for c in range(2):
                gu_chunk("glu", c, None, 2, 4, "glu" if c == 0 else None)
            on_partitions("conv", 2)
            sum_squares("ssm", 4, 3, tmp[:, 4:8, :])
            on_partitions("ssm", 3, 1)
            project("w_out", 4, "ymix")
            sum_squares("ffn2", KD)
            on_partitions("ffn2")
            feed_forward("ffn2", NF, 2)
            sum_squares("final", KD)
            on_partitions("final")

            e.wait_ge(sem("zw_ok"), 1)
            e.wait_ge(x_ok, X_AT["a"])
            for k in range(KD):
                mm = e.matmul(ps[0:16, 7, 0:S], zw[:, k, :], x_t[:, k, :], start=(k == 0), stop=(k == KD - 1))
            mm.then_inc(sem("z"), 1)
            gu_chunk("a_qk", 0, first="a")
            sum_squares("a", KD)
            on_partitions("a")
            gu_chunk("a_qk", 1)
            e.wait_ge(sem("z_ok"), 1)
            for h in range(GH):
                mm = e.matmul(acc_tile(h), gup[:, h * P:(h + 1) * P], z_sb[:, :], start=True, stop=True,
                              skip_group_check=True)
            mm.then_inc(sem("gate_in"), 1)
            gu_chunk("a_qk", 2)
            gu_chunk("a_qk", 3)
            e.wait_ge(sem("gate_read"), 2)
            rows_product("a_v")
            gu_chunk("a_g", 0)
            gu_chunk("a_g", 1)
            e.wait_ge(sem("qdec"), 1)
            e.wait_ge(sem("v_rows_a"), 1)
            off = 0
            for b in range(NBLK):
                n = GBLK * (b + 1)
                e.wait_ge(sem("kdec"), b + 1)
                for h in range(GH):
                    for jt in range(1 + (b >= 4)):
                        m = min(P, n - jt * P)
                        at = off + h * n + jt * P
                        mm = e.matmul(ps[0:m, 2 + 2 * jt + h // 2, (h % 2) * S + b * GBLK:(h % 2) * S + (b + 1) * GBLK],
                                      k_dec[:, at:at + m], q_dec[:, h * S + b * GBLK:h * S + (b + 1) * GBLK],
                                      start=True, stop=True, skip_group_check=True)
                off += GH * n
            mm.then_inc(sem("att"), 1)
            gu_chunk("a_g", 2)
            e.wait_ge(sem("at_sb"), 9)
            for h in range(GH):
                for vh in range(2):
                    t = 2 * h + vh
                    dst = ps[:, 2 + t // 2, (t % 2) * S:(t % 2 + 1) * S]
                    cols = slice(h * GDV + vh * P, h * GDV + (vh + 1) * P)
                    e.matmul(dst, v_rows[:, 0, cols], at_sb[:, h * S:(h + 1) * S], start=True, stop=False,
                             skip_group_check=True)
                    mm = e.matmul(dst[:, P:S], v_rows[:, 1, cols], at_sb[:, 1024 + h * S + P:1024 + (h + 1) * S],
                                  start=False, stop=True, skip_group_check=True)
            mm.then_inc(sem("o_a"), 1)
            gu_chunk("a_g", 3)
            e.wait_ge(sem("osq_a"), 1)
            osq = tiles(k_dec[:, 0:2048])
            for t in range(2):
                for h in range(GH):
                    for vh in range(2):
                        mm = e.matmul(ps[:, 6, t * GH + h:t * GH + h + 1], osq[:, 2 * h + vh, t * P:(t + 1) * P],
                                      ones[:, 0:1], start=(vh == 0), stop=(vh == 1), skip_group_check=True)
            mm.then_inc(sem("oss_a"), 1)
            e.wait_ge(sem("or_a"), 1)
            for h in range(GH):
                for t in range(2):
                    at = (h % 2) * S + t * P
                    mm = e.matmul(ps[:, h // 2, at:at + P], st_s[:, 0, 16 + t * GH + h:17 + t * GH + h]
                                  .to_broadcast([P, P]), ident[:, :], start=True, stop=True, skip_group_check=True)
            mm.then_inc(sem("orb_a"), 1)
            project("a_out", 4, "oa")
            feed_forward("mlp0", NHID, 1)

            gu_chunk("b_k", 0, first="kv")
            sum_squares("kv", KD)
            on_partitions("kv")
            for c in range(1, 4):
                gu_chunk("b_k", c)
            rows_product("b_v")
            gu_chunk("b_q", 0, first="b")

            def component_squares(name, sq):
                for t in range(2):
                    for h in range(DH):
                        at = (t * DH + h) * 2
                        mm = e.matmul(ps[:, 6, at:at + 2], sq[:, h, t * P:(t + 1) * P], ones_2[:, :], start=True,
                                      stop=True, skip_group_check=True)
                mm.then_inc(sem(name + "ss"), 1)

            def component_norms(name, r):
                e.wait_ge(sem(name + "r"), 1)
                for h in range(DH):
                    for t in range(2):
                        for c in range(2):
                            at = (t * DH + h) * 2 + c
                            mm = e.matmul(acc_tile(h)[c * DD:(c + 1) * DD, t * P:(t + 1) * P],
                                          r[:, at:at + 1].to_broadcast([P, DD]), ident[:, :], start=True, stop=True,
                                          skip_group_check=True)
                mm.then_inc(sem(name + "rb"), 1)

            e.wait_ge(sem("masks"), 5)
            e.wait_ge(sem("ksq"), 1)
            component_squares("k", tmp)
            gu_chunk("b_q", 1)
            e.wait_ge(sem("v_rows_b"), 1)
            component_norms("k", k_r)
            gu_chunk("b_q", 2)
            gu_chunk("b_q", 3)
            e.wait_ge(sem("qsq"), 1)
            component_squares("q", tmp)
            e.wait_ge(sem("k_n"), 1)
            component_norms("q", q_r)
            e.wait_ge(sem("q_n"), 1)

            def scores(h):
                b = 2 * (h % 3)
                if h >= 3:
                    e.wait_ge(sem("p_exp"), 4 * (h - 2))
                for c in range(2):
                    rows = slice(DD * c, DD * c + DD)
                    for at, q, k, diagonal in ((0, 0, 0, True), (P, P, 0, False), (2 * P, P, P, True)):
                        dst = ps[:, b + c, at:at + P]
                        if diagonal:
                            e.matmul(dst, ident_b[:, :], mask_b[:, :], start=True, stop=False, skip_group_check=True)
                        mm = e.matmul(dst, q_n[rows, h, q:q + P], k_n[rows, h, k:k + P], start=not diagonal, stop=True,
                                      skip_group_check=True)
                mm.then_inc(sem("scores"), 1)

            def turn(h):
                at = (h % 2) * 384
                e.wait_ge(sem("a_ok"), 2 * (h + 1))
                if h >= 1:
                    e.wait_ge(sem("a_t"), h)
                for q in range(3):
                    mm = e.transpose(ps[:, 6, q * P:(q + 1) * P], a_sb[:, at + q * P:at + (q + 1) * P], ident[:, :])
                mm.then_inc(sem("a_turned"), 1)

            def weigh(h):
                at = (h % 2) * 384
                e.wait_ge(sem("a_t"), h + 1)
                if h >= 1:
                    e.wait_ge(sem("osq_b"), h)
                dst = ps[:, 7, 0:S]
                e.matmul(dst, v_rows[:, 0, h * P:(h + 1) * P], a_t[:, at:at + S], start=True, stop=False,
                         skip_group_check=True)
                e.matmul(dst[:, P:S], v_rows[:, 1, h * P:(h + 1) * P], a_t[:, at + S:at + S + P], start=False,
                         stop=True, skip_group_check=True).then_inc(sem("o_b"), 1)

            scores(0)
            scores(1)
            for h in range(DH):
                if h + 2 < DH:
                    scores(h + 2)
                turn(h)
                weigh(h)
            e.wait_ge(sem("osq_b"), DH)
            e.wait_ge(sem("a_t"), DH)
            for t in range(2):
                for h in range(DH):
                    mm = e.matmul(ps[:, 6, t * DH + h:t * DH + h + 1], tmp[:, h, t * P:(t + 1) * P], ones[:, 0:1],
                                  start=True, stop=True, skip_group_check=True)
            mm.then_inc(sem("oss_b"), 1)
            e.wait_ge(sem("or_b"), 1)
            for h in range(DH):
                for t in range(2):
                    mm = e.matmul(acc_tile(h)[:, t * P:(t + 1) * P],
                                  st_s[:, 0, 16 + t * DH + h:17 + t * DH + h].to_broadcast([P, P]), ident[:, :],
                                  start=True, stop=True, skip_group_check=True)
                if h % 2 == 1:
                    mm.then_inc(sem("orb_b"), 1)
            project("b_out", 4, "ob")
            feed_forward("mlp1", NHID, 1)
            for t in range(2):
                for k in range(KD):
                    if t == 0:
                        e.wait_ge(x_ok, X_AT["mlp1"] + k + 1)
                    bank = (6 + k // 4) if t == 0 else k // 4
                    mm = e.transpose(ps[:, bank, (k % 4) * P:(k % 4 + 1) * P], x_t[:, k, t * P:(t + 1) * P], ident[:, :])
                    if k % 4 == 3:
                        mm.then_inc(sem("x_turned"), 1)

        @block.scalar
        def _(e):
            def act(dst, src, f, **kw):
                return e.activation(dst, src, f, **kw)

            def squares(name, src, n, dst=None, x_at=None):
                dst = tmp if dst is None else dst
                for q in range(n // 2):
                    if x_at is not None:
                        e.wait_ge(x_ok, x_at(2 * q + 1))
                    act(dst[:, 2 * q:2 * q + 2, :], src[:, 2 * q:2 * q + 2, :], ACT.Square).then_inc(sem("sq"), 1)

            def roots(name, n, bank=6, slot=0):
                e.wait_ge(sem("ss"), after("ss", name, 1))
                act(root_t[:, slot, :], ps[:, bank, 0:2], ACT.Sqrt, scale=1.0 / n, bias=eps[:, 0:1])\
                    .then_inc(sem("root"), 1)

            def late(name, n=D):
                roots(name, n)
                e.wait_ge(sem("rb"), after("rb", name, 1))
                act(rs[:, :], ps[:, 6, S:2 * S], ACT.Copy).then_inc(sem("rs"), 1)

            def x_count(name):
                prev, each = X_FROM[name]
                return lambda k: X_AT[name] - prev + k // each + 1

            def gained(name, gain, first=None):
                at = x_count(name)
                for k in range(KD):
                    e.wait_ge(x_ok, at(k))
                    if first and k == 0:
                        e.wait_ge(*first)
                    act(h_hi[:, k, :], x_t[:, k, :], ACT.Copy, scale=gain(k)).then_inc(sem("hh"), 1)

            def h_his(name, src, n, shift=None):
                for k in range(n):
                    e.wait_ge(sem("t"), after("t", name, k + 1))
                    if shift is None:
                        act(h_hi[:, k, :], src[:, k, :], ACT.Copy).then_inc(sem("hh"), 1)
                    else:
                        act(h_hi[:, k, :], src[:, k, :], ACT.Identity, bias=shift(k)).then_inc(sem("hh"), 1)

            def norm(name, shift=None):
                squares(name, x_t, KD, None, x_count(name))
                roots(name, D)
                h_his(name, tmp, KD, shift)

            def feed_forward(stage, n):
                glu = stage.startswith("ffn")
                ab, db, gb = A_BASE[stage], D_BASE[stage], GU_BASE[stage]

                def step(f, i):
                    slot = (db + f) % 2
                    if glu:
                        e.wait_ge(a_used, lin(ab + f + 1, i, 2))
                        if i is not None or db + f >= 2:
                            e.wait_ge(gu_free, lin(gb + f - 1, i, 2))
                        act(gate[:, slot, :], ps[:, (gb + f) % 2, 0:S], ACT.Silu).then_inc(gated, 1)
                    if i is not None:
                        hi_split_a(e, ab + f + 2, i, A_SIZE[stage])
                    else:
                        ahead(hi_split_a, e, stage, f)
                    e.wait_ge(gu_free, lin(gb + f + 1, i, 2))
                    if i is not None or db + f >= 2:
                        e.wait_ge(d_used, lin(db + f - 1, i, 2))
                    if glu:
                        act(hid_hi[:, slot, :], hid[:, slot, :], ACT.Copy).then_inc(hid_hi_ok, 1)
                    else:
                        if i is not None or f >= 2:
                            e.wait_ge(hid_ok, lin(db + f - 1, i, 2))
                        act(hid[:, slot, :], gate[:, slot, :], ACT.Square).then_inc(gated, 1)
                        act(hid_hi[:, slot, :], gate[:, slot, :], ACT.Square).then_inc(hid_hi_ok, 1)
                    if i is not None or f >= 1:
                        hi_split_d(e, db + f + 1, i)

                if stage in LATE:
                    squares(stage, x_t, KD)
                    late(stage)
                feed_forward_steps(e, n, step)

            e.dma_start(v0_rows[0:72, :], T["b_mod"][0].rearrange("(r c) -> r c", c=P)).then_inc(sem("ld_v0"), 16)
            e.dma_start(v0_rows[72:80, :], T["cond"][0].rearrange("(r c) -> r c", c=P)).then_inc(sem("ld_v0"), 16)
            e.dma_start(arena[:, 0:2 * D].rearrange("p (t n) -> p t n", t=2),
                        T["x"][0].rearrange("(t p) n -> p t n", p=P)).then_inc(sem("ld_x"), 16)
            e.wait_ge(sem("t_v0"), 1)
            act(cact[:, :], ps[:, 6, 72:80], ACT.Silu).then_inc(sem("cact"), 1)
            act(v0[:, :], ps[:, 6, 0:80], ACT.Copy).then_inc(sem("v0_ok"), 1)
            e.wait_ge(sem("t_x"), 1)
            for q in range(2):
                act(x_t[:, 4 * q:4 * q + 4, :], acc4[:, 1024 * q:1024 * (q + 1)], ACT.Copy).then_inc(x_ok, 1)
            e.wait_ge(sem("eps_ok"), 1)
            e.wait_ge(x_ok, 2)
            squares("ffn1", x_t, KD)
            roots("ffn1", D)
            e.wait_ge(sem("t_v1"), 1)
            act(v1[:, :], ps[:, 0, 0:V1_N], ACT.Copy).then_inc(sem("v12_ok"), 1)
            e.wait_ge(sem("t_v2"), 1)
            act(v2[:, :], ps[:, 1, 0:V2_N], ACT.Copy).then_inc(sem("v12_ok"), 1)
            e.wait_ge(sem("ld_dt"), 32)
            act(dt_col[:, :], dt_col[:, :], ACT.Exp).then_inc(sem("dt"), 1)
            e.wait_ge(sem("s5_args"), 1)
            act(s5[:, 2, :], s5[:, 0, :], ACT.Exp).then_inc(sem("s5_mag"), 1)
            e.wait_ge(sem("s5_red"), 2)
            act(s5[:, 3, :], s5[:, 6, :], ACT.Sin).then_inc(sem("s5_trig"), 1)
            act(s5[:, 4, :], s5[:, 7, :], ACT.Sin).then_inc(sem("s5_trig"), 1)
            hi_split_a(e, 0)
            hi_split_a(e, 1)
            hi_split_d(e, 0)
            hi_split_d(e, 1)
            h_his("ffn1", tmp, KD, lambda k: mod[:, k:k + 1])
            feed_forward("ffn1", NF)

            for q, (dst, bank, scale) in enumerate(((b_t[:, 0], 6, 1.0), (b_t[:, 1], 0, 1.0), (c_t[:, 0], 1, 1.0),
                                                    (c_t[:, 1], 1, -1.0), (c_t[:, 2], 6, -1.0))):
                e.wait_ge(sem("bc_t"), (1, 2, 3, 3, 4)[q])
                act(dst, ps[:, bank, :].rearrange("p (u n) -> p u n", u=4), ACT.Copy, scale=scale)\
                    .then_inc(sem("bc_t_ok"), 1)
            norm("mix", lambda k: mod[:, 3 * KD + k:3 * KD + k + 1])
            hi_split_d(e, NF + 1)
            for c in range(8):
                e.wait_ge(a_used, A_BASE["w_in"] + c + 1)
                t0 = WIN_TILES[2 * c]
                act(proj[:, t0:t0 + 2, :], ps[:, (GU_BASE["w_in"] + c) % 2, :], ACT.Copy).then_inc(gu_free, 1)
                ahead(hi_split_a, e, "w_in", c)
            for u in range(4):
                e.wait_ge(sem("y_pre"), u + 1)
                act(y_ssm[:, u, :], y_ssm[:, u, :], ACT.Gelu_apprx_tanh).then_inc(sem("gelu"), 1)
                e.wait_ge(sem("gelu"), u + 1)
                act(h_hi[:, u, :], y_ssm[:, u, :], ACT.Copy).then_inc(sem("hh"), 1)
            e.wait_ge(sem("conv_ok"), 7)
            squares("conv", proj[:, 0:4, :], 4)
            roots("conv", 512, 2)
            for c in range(2):
                e.wait_ge(a_used, A_BASE["glu"] + c + 1)
                for a in range(2):
                    t = 2 * c + a
                    ins = act(proj[:, 12 + t, :], ps[:, (GU_BASE["glu"] + c) % 2, a * S:(a + 1) * S], ACT.Sigmoid,
                              bias=vec(v1, V1, "glu_b", t))
                ins.then_inc(gu_free, 1)
                ahead(hi_split_a, e, "glu", c)
            e.wait_ge(sem("glu_ok"), 1)
            squares("ssm", y_ssm, 4, tmp[:, 4:8, :])
            roots("ssm", 512, 3, 1)
            h_his("ymix", tmp, KD)
            for c in range(4):
                e.wait_ge(a_used, A_BASE["w_out"] + c + 1)
                ahead(hi_split_a, e, "w_out", c)
            norm("ffn2", lambda k: mod[:, 6 * KD + k:6 * KD + k + 1])
            feed_forward("ffn2", NF)
            squares("final", x_t, KD, None, x_count("final"))
            roots("final", D)

            gained("a", lambda k: vec(v1, V1, "a_norm_2", k))
            hi_split_d(e, 2 * NF + 1)
            squares("a", x_t, KD)
            late("a")
            mag = area(8192, 1024)
            for c in range(2):
                ahead(hi_split_a, e, "a_qk", c)
            e.wait_ge(sem("gate_in"), 1)
            for h in range(GH):
                ins = act(mag[:, h * S:(h + 1) * S], acc4[:, h * S:(h + 1) * S], ACT.Abs,
                          bias=vec(v1, V1, "a_b_gate_2", h))
            ins.then_inc(sem("gate_read"), 1)
            e.wait_ge(sem("gate_read"), 1)
            act(mag, mag, ACT.Exp, scale=-1.0).then_inc(sem("gate_exp"), 1)
            e.wait_ge(sem("gate_exp"), 1)
            act(mag, mag, ACT.Ln, bias=1.0).then_inc(sem("gate_ln"), 1)
            for c in range(2, 4):
                ahead(hi_split_a, e, "a_qk", c)
            e.wait_ge(sem("q_arg"), 1)
            act(q_dec, q_dec, ACT.Exp, scale=1.0 / TAU).then_inc(sem("q_exp"), 1)
            for c in range(4):
                e.wait_ge(a_used, A_BASE["a_v"] + c + 1)
                ahead(hi_split_a, e, "a_v", c)
            for t in range(2):
                ins = act(v_rows[:, t, :], acc4[:, t * 1024:(t + 1) * 1024], ACT.Copy, scale=r_tok[:, 0, t:t + 1])
            ins.then_inc(sem("v_rows_a"), 1)
            off = 0
            for b in range(NBLK):
                n = GH * GBLK * (b + 1)
                e.wait_ge(sem("k_arg"), b + 1)
                act(k_dec[:, off:off + n], k_dec[:, off:off + n], ACT.Exp, scale=1.0 / TAU).then_inc(sem("k_exp"), 1)
                off += n
            def output_gates(c):
                e.wait_ge(gu_free, GU_BASE["a_g"] + c + 1)
                act(silu_g[:, 2 * c:2 * c + 2, :], silu_g[:, 2 * c:2 * c + 2, :], ACT.Silu).then_inc(sem("g_ok"), 1)

            for c in range(3):
                ahead(hi_split_a, e, "a_g", c)
                output_gates(c)
            e.wait_ge(sem("o_a"), 1)
            act(k_dec[:, 0:2048], acc4, ACT.Square).then_inc(sem("osq_a"), 1)
            ahead(hi_split_a, e, "a_g", 3)
            output_gates(3)
            e.wait_ge(sem("oss_a"), 1)
            act(st_s[:, 0, 0:8], ps[:, 6, 0:8], ACT.Sqrt, scale=1.0 / GDV, bias=eps[:, 0:1]).then_inc(sem("oroot_a"), 1)
            h_his("oa", tmp, KD)
            for c in range(4):
                e.wait_ge(a_used, A_BASE["a_out"] + c + 1)
                ahead(hi_split_a, e, "a_out", c)
            gained("mlp0", lambda k: vec(v1, V1, "mlp_norm_2", k), (a_used, A_BASE["a_out"] + 4))
            feed_forward("mlp0", NHID)

            gained("kv", lambda k: vec(v1, V1, "kv_norm_2", k))
            hi_split_d(e, 2 * NF + NHID + 1)
            squares("kv", x_t, KD)
            late("kv")
            for c in range(4):
                ahead(hi_split_a, e, "b_k", c)
            for c in range(4):
                ahead(hi_split_a, e, "b_v", c)
                e.wait_ge(a_used, A_BASE["b_v"] + c + 1)
                for k in (2 * c, 2 * c + 1):
                    act(h_hi[:, k, :], x_t[:, k, :], ACT.Copy, scale=vec(v1, V1, "b_norm_2", k)).then_inc(sem("hh"), 1)
            for t in range(2):
                ins = act(v_rows[:, t, :], acc4[:, t * 1024:(t + 1) * 1024], ACT.Copy, scale=r_tok[:, 0, t:t + 1])
            ins.then_inc(sem("v_rows_b"), 1)
            e.wait_ge(gu_free, GU_BASE["b_k"] + 4)
            act(tmp_flat, area(0, 2048), ACT.Square).then_inc(sem("ksq"), 1)
            e.wait_ge(sem("kss"), 1)
            act(k_r[:, :], ps[:, 6, 0:32], ACT.Sqrt, scale=1.0 / DD, bias=eps[:, 0:1]).then_inc(sem("kroot"), 1)
            for c in range(4):
                ahead(hi_split_a, e, "b_q", c)
            e.wait_ge(gu_free, GU_BASE["b_q"] + 4)
            act(tmp_flat, area(4096, 2048), ACT.Square).then_inc(sem("qsq"), 1)
            e.wait_ge(sem("qss"), 1)
            act(q_r[:, :], ps[:, 6, 0:32], ACT.Sqrt, scale=1.0 / DD, bias=eps[:, 0:1]).then_inc(sem("qroot"), 1)
            e.wait_ge(sem("lam_dots"), 1)
            act(lam_s[:, 2:4], lam_s[:, 0:2], ACT.Exp).then_inc(sem("lam_exp"), 1)
            def exponentials(h):
                hb, bank = h % 2, 2 * (h % 3)
                e.wait_ge(sem("s_max"), 2 * (h + 1))
                if h >= 2:
                    e.wait_ge(sem("a_ok"), 2 * (h - 1))
                for c in range(2):
                    for q in range(2):
                        at = hb * 768 + c * 384 + (P if q else 0)
                        o, n = (P, S) if q else (0, P)
                        act(p_sb[:, at:at + n], ps[:, bank + c, o:o + n], ACT.Exp,
                            bias=st_s[:, hb, 2 * q + c:2 * q + c + 1],
                            accum_out=st_s[:, hb, 4 + 2 * q + c:5 + 2 * q + c]).then_inc(sem("p_exp"), 1)

            def output(h):
                e.wait_ge(sem("o_b"), h + 1)
                act(o_b[:, h, :], ps[:, 7, 0:S], ACT.Copy).then_inc(sem("o_copy"), 1)
                act(tmp[:, h, :], ps[:, 7, 0:S], ACT.Square).then_inc(sem("osq_b"), 1)

            for h in range(DH):
                exponentials(h)
                if h >= 1:
                    output(h - 1)
            output(DH - 1)
            e.wait_ge(sem("oss_b"), 1)
            act(st_s[:, 0, 0:16], ps[:, 6, 0:16], ACT.Sqrt, scale=1.0 / P, bias=eps[:, 0:1]).then_inc(sem("oroot_b"), 1)
            h_his("ob", tmp, KD)
            for c in range(4):
                e.wait_ge(a_used, A_BASE["b_out"] + c + 1)
                ahead(hi_split_a, e, "b_out", c)
            gained("mlp1", lambda k: vec(v1, V1, "mlp_norm_2", KD + k), (a_used, A_BASE["b_out"] + 4))
            feed_forward("mlp1", NHID)
            for t in range(2):
                for q in range(2):
                    if (2 * t + q) % 2 == 0:
                        e.wait_ge(sem("x_turned"), 2 * t + q + 1)
                        bank = (6 + q) if t == 0 else q
                        act(arena[:, t * D + q * 512:t * D + (q + 1) * 512], ps[:, bank, :], ACT.Copy)\
                            .then_inc(sem("out_rows"), 1)

        @block.vector
        def _(e):
            def h_los(name, src, n, shift=None):
                for k in range(n):
                    e.wait_ge(sem("hh"), after("hh", name, k + 1))
                    hi = h_hi[:, k, :].bitcast(F32)
                    if shift is None:
                        ins = e.tensor_tensor(h_lo[:, k, :], src[:, k, :], hi, ALU.subtract)
                    else:
                        ins = e.scalar_tensor_tensor(out=h_lo[:, k, :], in0=src[:, k, :], scalar=shift(k), in1=hi,
                                                     op0=ALU.add, op1=ALU.subtract)
                    ins.then_inc(sem("h"), 1)

            def token_norms(name, slot=0):
                e.wait_ge(sem("root"), after("root", name, 1))
                e.reciprocal(r_tok[:, slot, :], root_t[:, slot, :]).then_inc(sem("rtok"), 1)

            def scaled(name, k, scale):
                if k == 0:
                    e.wait_ge(sem("rb"), after("rb", name, 1))
                e.scalar_tensor_tensor(out=tmp[:, k, :], in0=x_t[:, k, :], scalar=scale(k), in1=ps[:, 6, S:2 * S],
                                       op0=ALU.mult, op1=ALU.mult).then_inc(sem("t"), 1)

            def low(name, k, shift):
                e.wait_ge(sem("hh"), after("hh", name, k + 1))
                e.scalar_tensor_tensor(out=h_lo[:, k, :], in0=tmp[:, k, :], scalar=shift(k),
                                       in1=h_hi[:, k, :].bitcast(F32), op0=ALU.add, op1=ALU.subtract)\
                    .then_inc(sem("h"), 1)

            def gained_low(name, k, gain):
                e.wait_ge(sem("hh"), after("hh", name, k + 1))
                e.scalar_tensor_tensor(out=h_lo[:, k, :], in0=x_t[:, k, :], scalar=gain(k),
                                       in1=h_hi[:, k, :].bitcast(F32), op0=ALU.mult, op1=ALU.subtract)\
                    .then_inc(sem("h"), 1)

            def norm(name, scale, shift):
                for k in range(KD + 1):
                    if k < KD:
                        scaled(name, k, scale)
                    if k >= 1:
                        low(name, k - 1, shift)

            def mod_chunk(m, i=None):
                slot = m % 2
                if m < MOD_WIDE:
                    e.wait_ge(sem(f"m_first{m}"), 16)
                else:
                    e.wait_ge(m_loaded[slot], lin(16 * ((m - MOD_WIDE) // 2 + 1), i, 16))
                w = mod_slot(m)
                if i is not None or m >= 2:
                    e.wait_ge(sem("m_done"), lin(m - 1, i, 2))
                for k in range(KD):
                    if k == 0:
                        ins = e.tensor_scalar(acc_m[:, slot, :], w[:, k, :], cact[:, k:k + 1], None, ALU.mult)
                    else:
                        e.wait_ge(m_step, lin(7 * m + k, i, 14))
                        ins = e.scalar_tensor_tensor(out=acc_m[:, slot, :], in0=w[:, k, :],
                                                     scalar=cact[:, k:k + 1], in1=acc_m[:, slot, :],
                                                     op0=ALU.mult, op1=ALU.add)
                    if k < KD - 1:
                        ins.then_inc(m_step, 1)
                ins.then_inc(m_summed, 1)

            def mod_columns(lo, hi, chunks, name):
                e.wait_ge(sem("m_done"), chunks)
                e.wait_ge(sem("v0_ok"), 1)
                e.tensor_tensor(mod[:, lo:hi], ps[:, 7, lo:hi], v0[:, lo:hi], ALU.add).then_inc(sem(name), 1)
                e.wait_ge(sem(name), 1)

            def norm_scale(n, section, gain):
                e.scalar_tensor_tensor(out=nscale[:, n, :], in0=mod[:, section * KD:(section + 1) * KD], scalar=1.0,
                                       in1=vec(v1, V1, gain, 0, KD), op0=ALU.add, op1=ALU.mult)\
                    .then_inc(sem(f"nscale{n}"), 1)
                e.wait_ge(sem(f"nscale{n}"), 1)

            def feed_forward(stage, n):
                ab, db, gb = A_BASE[stage], D_BASE[stage], GU_BASE[stage]
                glu = stage.startswith("ffn")
                up = S
                if not glu:
                    token_norms(stage)
                    e.wait_ge(sem("rs"), 1 + LATE.index(stage))

                def step(f, i):
                    slot = (db + f) % 2
                    if glu:
                        e.wait_ge(gated, lin(db + f + 1, i, 2))
                        e.tensor_tensor(hid[:, slot, :], gate[:, slot, :], ps[:, (gb + f) % 2, up:up + S], ALU.mult)\
                            .then_inc(gu_free, 1)
                    else:
                        e.wait_ge(a_used, lin(ab + f + 1, i, 2))
                        e.scalar_tensor_tensor(out=gate[:, slot, :], in0=ps[:, (gb + f) % 2, 0:S], scalar=0.0,
                                               in1=rs[:, :], op0=ALU.max, op1=ALU.mult).then_inc(gu_free, 1)
                    if stage == "ffn1" and (i is not None or f < n - 1):
                        if f == n - 3:
                            mod_columns(2 * KD, 6 * KD, MOD0 + 1 + f, "mod_b")
                        mod_chunk(MOD0 + 1 + f, i)
                    if stage == "ffn2" and i is None and f in MOD_FFN2:
                        mod_chunk(MOD_FFN2[f])
                    if i is not None:
                        lo_split_a(e, ab + f + 2, i, A_SIZE[stage])
                    else:
                        ahead(lo_split_a, e, stage, f)
                    e.wait_ge(hid_hi_ok, lin(db + f + 1, i, 2))
                    e.tensor_tensor(hid_lo[:, slot, :], hid[:, slot, :], hid_hi[:, slot, :].bitcast(F32), ALU.subtract)\
                        .then_inc(hid_ok, 1)
                    if i is not None or f >= 1:
                        lo_split_d(e, db + f + 1, i)
                feed_forward_steps(e, n, step)

            def add_down(stage, scale, then=None):
                for k in range(KD + 1):
                    if k < KD:
                        if k == 6:
                            e.wait_ge(d_used, D_BASE[stage] + dict(D_STAGES)[stage])
                        elif k % 2 == 0:
                            e.wait_ge(sem("acc_ok"), 3 * list(D_BASE).index(stage) + k // 2 + 1)
                        if scale is None:
                            ins = e.tensor_tensor(x_t[:, k, :], x_t[:, k, :], acc_tile(k), ALU.add)
                        else:
                            ins = e.scalar_tensor_tensor(out=x_t[:, k, :], in0=acc_tile(k), scalar=scale(k),
                                                         in1=x_t[:, k, :], op0=ALU.mult, op1=ALU.add)
                        ins.then_inc(x_ok, 1)
                    if then and k >= 1:
                        then(k - 1)

            def ssm_parameters():
                e.wait_ge(sem("dt"), 1)
                c5 = [0]

                def s5_step(ins):
                    c5[0] += 1
                    ins.then_inc(sem("s5_step"), 1)
                    e.wait_ge(sem("s5_step"), c5[0])

                lre, lim = vec(v2, V2, "lambda_re", 0, ST), vec(v2, V2, "lambda_im", 0, ST)
                s5_step(e.tensor_tensor(s5[:, 0, :], lre, dt_col[:, :], ALU.mult))
                e.tensor_tensor(s5[:, 1, :], lim, dt_col[:, :], ALU.mult).then_inc(sem("s5_args"), 1)
                e.wait_ge(sem("s5_args"), 1)
                for row, shift in ((6, 0.25), (7, 0.0)):
                    s5_step(e.tensor_scalar(s5[:, 5, :], s5[:, 1, :], 1.0 / (2 * math.pi), shift, ALU.mult, ALU.add))
                    s5_step(e.tensor_scalar(s5[:, 5, :], s5[:, 5, :], ROUND, ROUND, ALU.add, ALU.subtract))
                    s5_step(e.scalar_tensor_tensor(out=s5[:, row, :], in0=s5[:, 5, :], scalar=-6.28125, in1=s5[:, 1, :],
                                                   op0=ALU.mult, op1=ALU.add))
                    rest = 2 * math.pi - 6.28125
                    s5_step(e.scalar_tensor_tensor(out=s5[:, row, :], in0=s5[:, 5, :], scalar=-rest, in1=s5[:, row, :],
                                                   op0=ALU.mult, op1=ALU.add))
                    s5_step(e.tensor_scalar(s5[:, row, :], s5[:, row, :], 2 * math.pi * shift, 3.1415925, ALU.add, ALU.min))
                    e.tensor_scalar(s5[:, row, :], s5[:, row, :], -3.1415925, None, ALU.max).then_inc(sem("s5_red"), 1)
                    e.wait_ge(sem("s5_red"), 1 if row == 6 else 2)
                e.wait_ge(sem("s5_trig"), 2)
                e.wait_ge(sem("s5_mag"), 1)
                s5_step(e.tensor_tensor(s5[:, 10, :], s5[:, 2, :], s5[:, 3, :], ALU.mult))
                s5_step(e.tensor_tensor(s5[:, 11, :], s5[:, 2, :], s5[:, 4, :], ALU.mult))
                s5_step(e.tensor_scalar(s5[:, 10, :], s5[:, 10, :], -1.0, None, ALU.add))
                s5_step(e.tensor_tensor(s5[:, 12, :], lre, lre, ALU.mult))
                s5_step(e.tensor_tensor(s5[:, 13, :], lim, lim, ALU.mult))
                s5_step(e.tensor_tensor(s5[:, 12, :], s5[:, 12, :], s5[:, 13, :], ALU.add))
                s5_step(e.reciprocal(s5[:, 12, :], s5[:, 12, :]))
                s5_step(e.tensor_tensor(s5[:, 8, :], s5[:, 10, :], lre, ALU.mult))
                s5_step(e.tensor_tensor(s5[:, 13, :], s5[:, 11, :], lim, ALU.mult))
                s5_step(e.tensor_tensor(s5[:, 8, :], s5[:, 8, :], s5[:, 13, :], ALU.add))
                s5_step(e.tensor_tensor(s5[:, 8, :], s5[:, 8, :], s5[:, 12, :], ALU.mult))
                s5_step(e.tensor_tensor(s5[:, 9, :], s5[:, 11, :], lre, ALU.mult))
                s5_step(e.tensor_tensor(s5[:, 13, :], s5[:, 10, :], lim, ALU.mult))
                s5_step(e.tensor_tensor(s5[:, 9, :], s5[:, 9, :], s5[:, 13, :], ALU.subtract))
                e.tensor_tensor(s5[:, 9, :], s5[:, 9, :], s5[:, 12, :], ALU.mult).then_inc(sem("s5_quot"), 1)

            e.memset(zero_w[:, :].bitcast(F32), 0.0).then_inc(sem("zero_ok"), 1)
            e.memset(eps[:, :], EPS).then_inc(sem("eps_ok"), 1)
            e.wait_ge(sem("cact"), 1)
            for m in range(MOD0):
                mod_chunk(m)
                if m == 1:
                    token_norms("ffn1")
                if m == 5:
                    e.wait_ge(sem("v12_ok"), 2)
                    ssm_parameters()
            lo_split_a(e, 0)
            lo_split_a(e, 1)
            mod_columns(0, 2 * KD, MOD0, "mod_a")
            norm_scale(0, 1, "ffn1_norm")
            norm("ffn1", lambda k: nscale[:, 0, k:k + 1], lambda k: mod[:, k:k + 1])
            lo_split_d(e, 0)
            lo_split_d(e, 1)
            mod_chunk(MOD0)
            feed_forward("ffn1", NF)
            e.tensor_scalar(ghalf[:, 0, :], mod[:, 2 * KD:3 * KD], 0.5, None, ALU.mult).then_inc(sem("ghalf0"), 1)
            norm_scale(1, 4, "mix_norm")
            e.wait_ge(sem("ghalf0"), 1)
            add_down("ffn1", lambda k: ghalf[:, 0, k:k + 1])

            token_norms("mix")
            norm("mix", lambda k: nscale[:, 1, k:k + 1], lambda k: mod[:, 3 * KD + k:3 * KD + k + 1])
            lo_split_d(e, NF + 1)
            mod_chunk(30)
            ahead(lo_split_a, e, "w_in", 0)
            mod_chunk(31)
            ahead(lo_split_a, e, "w_in", 1)
            e.wait_ge(sem("b_bd_ok"), 1)
            bu_re, bu_im = acc4[:, 0:1024], acc4[:, 1024:2048]

            def states(u):
                pr = ph_re[:, 4 * u:4 * u + 4, :].rearrange("p t n -> p (t n)")
                pi = ph_im[:, 4 * u:4 * u + 4, :].rearrange("p t n -> p (t n)")
                e.wait_ge(sem("bu"), u + 1)
                if u >= 1:
                    e.wait_ge(sem("y_ssm"), u)
                for q, (b, f) in enumerate(((bu_re, pr), (bu_im, pi), (bu_im, pr), (bu_re, pi))):
                    ins = e.tensor_tensor(prod[q], b, f, ALU.mult)
                ins.then_inc(sem("bu_read"), 1)
                e.wait_ge(sem("bu_read"), u + 1)
                e.tensor_tensor(w_re, prod[0], prod[1], ALU.add)
                e.tensor_tensor(w_im, prod[2], prod[3], ALU.subtract).then_inc(sem("demod"), 1)
                e.wait_ge(sem("demod"), u + 1)
                for w in (w_re, w_im):
                    for j in range(4):
                        part = w[:, j * S:(j + 1) * S]
                        ins = e.tensor_tensor_scan(part, s5[:, 2, 4 * u + j:4 * u + j + 1].to_broadcast([P, S]), part,
                                                   0.0, ALU.mult, ALU.add)
                ins.then_inc(sem("scanned"), 1)
                e.wait_ge(sem("scanned"), u + 1)
                for q, (f, w) in enumerate(((pr, w_re), (pi, w_im), (pr, w_im), (pi, w_re))):
                    e.tensor_tensor(prod[q], f, w, ALU.mult).then_inc(sem("remod"), 1)

            def skip(u):
                e.wait_ge(sem("y_ssm"), u + 1)
                e.scalar_tensor_tensor(out=y_ssm[:, u, :], in0=proj[:, 12 + u, :], scalar=vec(v1, V1, "ssm_d", u),
                                       in1=ps[:, 6, 0:S], op0=ALU.mult, op1=ALU.add).then_inc(sem("y_pre"), 1)

            for u in range(4):
                states(u)
                if u < 3:
                    ahead(lo_split_a, e, "w_in", 2 * u + 2)
                    ahead(lo_split_a, e, "w_in", 2 * u + 3)
                skip(u)
            for u in range(4):
                e.wait_ge(sem("hh"), after("hh", "glu", u + 1))
                e.tensor_tensor(h_lo[:, u, :], y_ssm[:, u, :], h_hi[:, u, :].bitcast(F32), ALU.subtract)\
                    .then_inc(sem("h"), 1)
            token_norms("conv")
            for c in range(2):
                ahead(lo_split_a, e, "glu", c)
            e.wait_ge(gu_free, GU_BASE["glu"] + 2)
            e.tensor_tensor(y_ssm, y_ssm, proj[:, 12:16, :], ALU.mult).then_inc(sem("glu_ok"), 1)
            token_norms("ssm", 1)
            for k in range(KD):
                if k % 4 == 0:
                    e.wait_ge(sem("rb"), after("rb", ("conv", "ssm")[k // 4], 1))
                src = proj[:, k, :] if k < 4 else y_ssm[:, k - 4, :]
                g = vec(v1, V1, "out_norm_conv", k) if k < 4 else vec(v1, V1, "out_norm_ssm", k - 4)
                e.scalar_tensor_tensor(out=tmp[:, k, :], in0=src, scalar=g, in1=ps[:, 2 + k // 4, S:2 * S], op0=ALU.mult,
                                       op1=ALU.mult).then_inc(sem("t"), 1)
            h_los("ymix", tmp, KD)

            def add_out(stage, scale=None):
                base = X_AT[{"w_out": "mix", "a_out": "a", "b_out": "b"}[stage]]
                for c in range(4):
                    bank = (GU_BASE[stage] + c) % 2
                    e.wait_ge(a_used, A_BASE[stage] + c + 1)
                    if scale is None:
                        e.tensor_tensor(x_t[:, 2 * c:2 * c + 2, :], x_t[:, 2 * c:2 * c + 2, :],
                                        ps[:, bank, :].rearrange("p (t n) -> p t n", t=2), ALU.add).then_inc(x_ok, 1)
                    else:
                        for a in range(2):
                            k = 2 * c + a
                            e.scalar_tensor_tensor(out=x_t[:, k, :], in0=ps[:, bank, a * S:(a + 1) * S],
                                                   scalar=scale(k), in1=x_t[:, k, :], op0=ALU.mult, op1=ALU.add)\
                                .then_inc(x_ok, 1)
                    e.wait_ge(x_ok, base + (c + 1) * (1 if scale is None else 2))
                    e.sem_inc(gu_free, 1)
                    ahead(lo_split_a, e, stage, c)

            add_out("w_out", lambda k: mod[:, 5 * KD + k:5 * KD + k + 1])
            mod_columns(6 * KD, 8 * KD, 32, "mod_c")
            norm_scale(2, 7, "ffn2_norm")
            token_norms("ffn2")
            norm("ffn2", lambda k: nscale[:, 2, k:k + 1], lambda k: mod[:, 6 * KD + k:6 * KD + k + 1])
            feed_forward("ffn2", NF)
            mod_columns(8 * KD, N_MOD * KD, 36, "mod_d")
            e.tensor_scalar(ghalf[:, 1, :], mod[:, 8 * KD:9 * KD], 0.5, None, ALU.mult).then_inc(sem("ghalf1"), 1)
            e.wait_ge(sem("ghalf1"), 1)
            add_down("ffn2", lambda k: ghalf[:, 1, k:k + 1])
            e.wait_ge(sem("ld_att"), 16 * 3)
            e.tensor_tensor(zw[:, :, :], zw[:, :, :], bcast(vec(v1, V1, "a_norm_2", 0, KD), 16), ALU.mult)\
                .then_inc(sem("zw_ok"), 1)
            token_norms("final")
            e.wait_ge(sem("rb"), after("rb", "final", 1))

            for k in range(KD + 1):
                if k < KD:
                    e.scalar_tensor_tensor(out=x_t[:, k, :], in0=x_t[:, k, :], scalar=vec(v1, V1, "final_norm", k),
                                           in1=ps[:, 6, S:2 * S], op0=ALU.mult, op1=ALU.mult).then_inc(x_ok, 1)
                if k >= 1:
                    gained_low("a", k - 1, lambda j: vec(v1, V1, "a_norm_2", j))
            lo_split_d(e, 2 * NF + 1)
            token_norms("a")

            def times_rms(stage, c, dst):
                e.wait_ge(a_used, A_BASE[stage] + c + 1)
                return e.tensor_tensor(dst[:, 2 * c:2 * c + 2, :], ps[:, (GU_BASE[stage] + c) % 2, :]
                                       .rearrange("p (t n) -> p t n", t=2),
                                       rs[:, :].unsqueeze(1).to_broadcast([P, 2, S]), ALU.mult).then_inc(gu_free, 1)

            e.wait_ge(sem("rs"), 1)
            e.wait_ge(sem("z"), 1)
            e.tensor_tensor(z_sb[:, :], ps[0:16, 7, 0:S], rs[0:16, :], ALU.mult).then_inc(sem("z_ok"), 1)
            for c in range(2):
                times_rms("a_qk", c, qk)
                ahead(lo_split_a, e, "a_qk", c)
            e.wait_ge(sem("gate_read"), 1)
            for h in range(GH):
                ins = e.tensor_scalar(cum[:, h * S:(h + 1) * S], acc4[:, h * S:(h + 1) * S],
                                      vec(v1, V1, "a_b_gate_2", h), 0.0, ALU.add, ALU.min)
            ins.then_inc(sem("gate_read"), 1)
            times_rms("a_qk", 2, qk)
            ahead(lo_split_a, e, "a_qk", 2)
            e.wait_ge(sem("gate_read"), 2)
            e.wait_ge(sem("gate_ln"), 1)
            mag = area(8192, 1024)
            e.tensor_tensor(cum, cum, mag, ALU.subtract).then_inc(sem("log_a"), 1)
            e.wait_ge(sem("log_a"), 1)
            for h in range(GH):
                part = cum[:, h * S:(h + 1) * S]
                ins = e.tensor_tensor_scan(part, ones[:, 0:1].to_broadcast([P, S]), part, 0.0, ALU.mult, ALU.add)
            ins.then_inc(sem("cum"), 1)
            times_rms("a_qk", 3, qk)
            ahead(lo_split_a, e, "a_qk", 3)
            e.wait_ge(sem("cum"), 1)
            cum_b = cum.rearrange("p (b n) -> p b n", n=GBLK)
            ref = cum_b[:, :, GBLK // 2 - 1]
            e.tensor_tensor(q_dec.rearrange("p (b n) -> p b n", n=GBLK), cum_b, bcast(ref, GBLK), ALU.subtract)\
                .then_inc(sem("q_arg"), 1)
            cum_h = cum.rearrange("p (h n) -> p h n", n=S)
            off = 0
            for b in range(NBLK):
                n = GBLK * (b + 1)
                at = b * GBLK + GBLK // 2 - 1
                dst = k_dec[:, off:off + GH * n].rearrange("p (h n) -> p h n", n=n)
                e.tensor_tensor(dst, bcast(cum_h[:, :, at], n), cum_h[:, :, 0:n], ALU.subtract).then_inc(sem("k_arg"), 1)
                off += GH * n
                if b % 2 == 1:
                    ahead(lo_split_a, e, "a_v", b // 2)
            e.memset(tmp_flat, 0.0).then_inc(sem("at_zero"), 1)
            e.wait_ge(sem("q_exp"), 1)
            e.wait_ge(gu_free, GU_BASE["a_qk"] + 4)
            e.scalar_tensor_tensor(out=q_dec, in0=area(0, 1024), scalar=float(GDK) ** -0.5, in1=q_dec, op0=ALU.mult,
                                   op1=ALU.mult).then_inc(sem("qdec"), 1)
            off = 0
            for b in range(NBLK):
                n = GBLK * (b + 1)
                dst = k_dec[:, off:off + GH * n].rearrange("p (h n) -> p h n", n=n)
                e.wait_ge(sem("k_exp"), b + 1)
                e.tensor_tensor(dst, dst, qk[:, 4:8, 0:n], ALU.mult).then_inc(sem("kdec"), 1)
                off += GH * n
            for c in range(2):
                times_rms("a_g", c, silu_g)
                ahead(lo_split_a, e, "a_g", c)
            e.wait_ge(sem("masks"), 5)
            e.wait_ge(sem("att"), 1)
            e.wait_ge(sem("at_zero"), 1)
            at4 = at_sb.rearrange("p (j h n) -> p j h n", j=2, h=GH)
            ap4 = acc4.rearrange("p (j h n) -> p j h n", j=2, h=GH)
            for b in range(NBLK):
                jt, m = b // 4, GBLK * (b % 4 + 1)
                i0 = b * GBLK
                mask = tri[0:m, i0 % P:i0 % P + GBLK].unsqueeze(1).to_broadcast([m, GH, GBLK])
                e.tensor_tensor(at4[0:m, jt, :, i0:i0 + GBLK], ap4[0:m, jt, :, i0:i0 + GBLK], mask, ALU.mult)\
                    .then_inc(sem("at_sb"), 1)
            e.tensor_copy(at4[:, 0, :, P:S], ap4[:, 0, :, P:S]).then_inc(sem("at_sb"), 1)
            for c in range(2, 4):
                times_rms("a_g", c, silu_g)
                ahead(lo_split_a, e, "a_g", c)
            e.wait_ge(sem("oroot_a"), 1)
            e.reciprocal(st_s[:, 0, 16:24], st_s[:, 0, 0:8]).then_inc(sem("or_a"), 1)
            e.wait_ge(sem("g_ok"), 4)
            e.wait_ge(sem("orb_a"), 1)
            for t in range(KD):
                h = t // 2
                e.scalar_tensor_tensor(out=silu_g[:, t, :], in0=silu_g[:, t, :],
                                       scalar=vec(v1, V1, "a_head_norm_2", t % 2),
                                       in1=ps[:, h // 2, (h % 2) * S:(h % 2 + 1) * S], op0=ALU.mult, op1=ALU.mult)\
                    .then_inc(sem("g_scaled"), 1)
            for t in range(KD):
                e.wait_ge(sem("g_scaled"), t + 1)
                e.tensor_tensor(tmp[:, t, :], acc4[:, t * S:(t + 1) * S], silu_g[:, t, :], ALU.mult)\
                    .then_inc(sem("t"), 1)
            h_los("oa", tmp, KD)
            add_out("a_out")
            for k in range(KD):
                gained_low("mlp0", k, lambda j: vec(v1, V1, "mlp_norm_2", j))
            feed_forward("mlp0", NHID)
            add_down("mlp0", None, lambda k: gained_low("kv", k, lambda j: vec(v1, V1, "kv_norm_2", j)))
            lo_split_d(e, 2 * NF + NHID + 1)

            token_norms("kv")
            e.wait_ge(sem("rs"), 3)
            for c in range(4):
                times_rms("b_k", c, k_n)
                ahead(lo_split_a, e, "b_k", c)
            for c in range(4):
                ahead(lo_split_a, e, "b_v", c)
                for k in (2 * c, 2 * c + 1):
                    gained_low("b", k, lambda j: vec(v1, V1, "b_norm_2", j))
            e.wait_ge(sem("kroot"), 1)
            e.reciprocal(k_r[:, :], k_r[:, :]).then_inc(sem("kr"), 1)
            for c in range(2):
                times_rms("b_q", c, q_n)
                ahead(lo_split_a, e, "b_q", c)
            e.wait_ge(sem("krb"), 1)
            e.scalar_tensor_tensor(out=area(0, 2048), in0=area(0, 2048), scalar=vec(v2, V2, "k_norm_2", 0),
                                   in1=acc4, op0=ALU.mult, op1=ALU.mult).then_inc(sem("k_n"), 1)
            for c in range(2, 4):
                times_rms("b_q", c, q_n)
                ahead(lo_split_a, e, "b_q", c)
            for a in range(2):
                e.tensor_tensor(st_lam[:, a, :], lamp[:, 2 * a, :], lamp[:, 2 * a + 1, :], ALU.mult)\
                    .then_inc(sem("lam_prod"), 1)
            e.wait_ge(sem("lam_prod"), 2)
            e.tensor_reduce(lam_s[:, 0:2], st_lam[:, :, :], AX.X, ALU.add).then_inc(sem("lam_dots"), 1)
            e.tensor_scalar(qgain[:, :], vec(v2, V2, "b_q_norm_2", 0), float(DD) ** -0.5, None, ALU.mult)\
                .then_inc(sem("qgain"), 1)
            e.wait_ge(sem("qroot"), 1)
            e.reciprocal(q_r[:, :], q_r[:, :]).then_inc(sem("qr"), 1)
            e.wait_ge(sem("qgain"), 1)
            e.wait_ge(sem("qrb"), 1)
            e.scalar_tensor_tensor(out=area(4096, 2048), in0=area(4096, 2048), scalar=qgain[:, 0:1], in1=acc4,
                                   op0=ALU.mult, op1=ALU.mult).then_inc(sem("q_n"), 1)
            e.wait_ge(sem("q_n"), 1)
            e.wait_ge(sem("lam_exp"), 1)
            e.tensor_tensor(lam_s[:, 4:5], lam_s[:, 3:4], lam_s[:, 2:3], ALU.subtract).then_inc(sem("lam_neg"), 1)
            e.wait_ge(sem("lam_neg"), 1)
            e.tensor_scalar(lam_s[:, 5:6], lam_s[:, 4:5], -LAM_INIT, None, ALU.add).then_inc(sem("lam_neg"), 1)

            def weights(h):
                hb = h % 2
                st = st_s[:, hb, :]
                e.wait_ge(sem("p_exp"), 4 * (h + 1))
                e.reciprocal(st[:, 8:12], st[:, 4:8]).then_inc(sem("p_rec"), 1)
                e.wait_ge(sem("p_rec"), h + 1)
                e.wait_ge(sem("lam_neg"), 2)
                e.tensor_scalar(st[:, 12:16], st[:, 8:12], lam_s[:, 5:6], None, ALU.mult).then_inc(sem("p_lam"), 1)
                e.wait_ge(sem("p_lam"), h + 1)
                if h >= 2:
                    e.wait_ge(sem("a_turned"), h - 1)
                for q in range(2):
                    n, o = (S, P) if q else (P, 0)
                    p0 = p_sb[:, hb * 768 + o:hb * 768 + o + n]
                    p1 = p_sb[:, hb * 768 + 384 + o:hb * 768 + 384 + o + n]
                    e.tensor_scalar(p1, p1, st[:, 13 + 2 * q:14 + 2 * q], None, ALU.mult).then_inc(sem("p1_ok"), 1)
                for q in range(2):
                    n, o = (S, P) if q else (P, 0)
                    p0 = p_sb[:, hb * 768 + o:hb * 768 + o + n]
                    p1 = p_sb[:, hb * 768 + 384 + o:hb * 768 + 384 + o + n]
                    e.wait_ge(sem("p1_ok"), 2 * h + q + 1)
                    e.scalar_tensor_tensor(out=a_sb[:, hb * 384 + o:hb * 384 + o + n], in0=p0,
                                           scalar=st[:, 8 + 2 * q:9 + 2 * q], in1=p1, op0=ALU.mult, op1=ALU.add)\
                        .then_inc(sem("a_ok"), 1)

            def turned(h):
                hb = h % 2
                e.wait_ge(sem("a_turned"), h + 1)
                if h >= 2:
                    e.wait_ge(sem("o_b"), h - 1)
                e.tensor_copy(a_t[:, hb * 384:(hb + 1) * 384], ps[:, 6, 0:384]).then_inc(sem("a_t"), 1)

            def maxima(h):
                hb, bank = h % 2, 2 * (h % 3)
                e.wait_ge(sem("scores"), h + 1)
                if h >= 2:
                    e.wait_ge(sem("p_exp"), 4 * (h - 1))
                for q, (o, n) in enumerate(((0, P), (P, S))):
                    e.tensor_reduce(st_s[:, hb, 2 * q:2 * q + 2], ps[:, bank:bank + 2, o:o + n], AX.X, ALU.max,
                                    negate=True).then_inc(sem("s_max"), 1)

            maxima(0)
            for h in range(DH):
                if h + 1 < DH:
                    maxima(h + 1)
                weights(h)
                turned(h)
            e.tensor_scalar(qgain[:, :], vec(v1, V1, "b_head_norm_2", 0), 1.0 - LAM_INIT, None, ALU.mult)\
                .then_inc(sem("qgain"), 1)
            e.wait_ge(sem("oroot_b"), 1)
            e.reciprocal(st_s[:, 0, 16:32], st_s[:, 0, 0:16]).then_inc(sem("or_b"), 1)
            e.wait_ge(sem("qgain"), 2)
            for t in range(KD):
                if t % 2 == 0:
                    e.wait_ge(sem("orb_b"), t // 2 + 1)
                e.scalar_tensor_tensor(out=tmp[:, t, :], in0=o_b[:, t, :], scalar=qgain[:, 0:1], in1=acc_tile(t),
                                       op0=ALU.mult, op1=ALU.mult).then_inc(sem("t"), 1)
            h_los("ob", tmp, KD)
            add_out("b_out")
            for k in range(KD):
                gained_low("mlp1", k, lambda j: vec(v1, V1, "mlp_norm_2", KD + j))
            feed_forward("mlp1", NHID)
            add_down("mlp1", None)
            for t in range(2):
                e.wait_ge(sem("x_turned"), 2 * t + 2)
                bank = 7 if t == 0 else 1
                e.tensor_copy(arena[:, t * D + 512:t * D + 1024], ps[:, bank, :]).then_inc(sem("out_rows"), 1)


        @block.gpsimd
        def _(e):
            e.memset(ident[:, :], 0.0).then_inc(sem("id0"), 1)
            e.memset(ones[:, :], 1.0).then_inc(sem("ones"), 1)
            e.wait_ge(sem("id0"), 1)
            e.affine_select(out=ident[:, :], in_=ident[:, :], compare_op=ALU.not_equal, fill=1.0, base=0,
                            pattern=[[-1, P]], channel_multiplier=1).then_inc(sem("ident_ok"), 1)
            for name, n in V1_ROWS:
                at = V1[name][0]
                src = T[name]
                if name == "conv_w":
                    v = src[0].rearrange("w (r c) -> (w r) c", c=P)
                elif name == "mlp_norm_2":
                    v = src.rearrange("l (r c) -> (l r) c", c=P)
                elif name in ("final_norm", "kv_norm_2"):
                    v = src.rearrange("(r c) -> r c", c=P)
                else:
                    v = src[0].rearrange("(r c) -> r c", c=P)
                e.dma_start(v1_rows[at:at + n, :], v).then_inc(sem("ld_v1"), 16)
            for name in ("lambda_re", "lambda_im"):
                at = V2[name][0]
                e.dma_start(v2_rows[at:at + ST, :], T[name][0].rearrange("(t g) n -> t (g n)", g=2))\
                    .then_inc(sem("ld_v2"), 16)
            for name in ("k_norm_2", "b_q_norm_2"):
                at = V2[name][0]
                src = T[name].rearrange("(a n) -> a n", a=1) if name == "k_norm_2" else T[name]
                for c in range(2):
                    e.dma_start(v2_rows[at:at + 1, c * DD:(c + 1) * DD], src).then_inc(sem("ld_v2"), 16)
            for g in range(2):
                e.dma_start(dt_col[g * NST:(g + 1) * NST, :],
                            T["log_dt"][0].rearrange("(t g) -> g t", g=2)[g:g + 1, :].to_broadcast([NST, ST]),
                            allow_slow_non_contiguous=True)\
                    .then_inc(sem("ld_dt"), 16)
            for r, name in enumerate(("ssm_b_re", "ssm_b_im")):
                e.dma_start(b_in[:, r], T[name][0].rearrange("(t g) n c -> (g n) t c", g=2))\
                    .then_inc(sem("ld_b"), 16)
            e.memset(c_in, 0.0).then_inc(sem("c_zero"), 1)
            e.memset(b_bd, 0.0).then_inc(sem("b_zero"), 1)
            e.wait_ge(sem("c_zero"), 1)
            for r, name in enumerate(("ssm_c_re", "ssm_c_im")):
                for a in range(8):
                    e.dma_start(c_in[a * GCH:(a + 1) * GCH, r, :, (a % 2) * NST:(a % 2 + 1) * NST],
                                T[name][0].rearrange("(u a) c n -> a c u n", a=8)[a])\
                        .then_inc(sem("ld_c"), 16)
            e.dma_start(zw[:, :, :], T["a_w_in_2"][0].rearrange("(k p) n -> p k n", p=P)[:, :, 3072:3088])\
                .then_inc(sem("ld_att"), 16)
            e.dma_start(gup[:, :], T["a_w_gate_up_2"][0]).then_inc(sem("ld_att"), 16)
            e.dma_start(lamp[:, :, :].rearrange("p a n -> p (a n)"),
                        T["b_lambda_2"].rearrange("l a n -> l (a n)").to_broadcast([P, 4 * DD]))\
                .then_inc(sem("ld_att"), 16)
            e.memset(ones_2[:, :], 0.0).then_inc(sem("blk"), 1)
            e.memset(tri[:, :], 0.0).then_inc(sem("blk"), 1)
            e.wait_ge(sem("blk"), 2)
            e.memset(ones_2[0:DD, 0:1], 1.0).then_inc(sem("masks"), 1)
            e.memset(ones_2[DD:P, 1:2], 1.0).then_inc(sem("masks"), 1)
            e.wait_ge(sem("masks"), 2)
            e.affine_select(out=tri[:, :], in_=tri[:, :], compare_op=ALU.is_ge, fill=MASKED, base=0,
                            pattern=[[-1, P]], channel_multiplier=1).then_inc(sem("blk"), 1)
            e.wait_ge(sem("blk"), 3)
            e.tensor_copy(mask_b[:, :], tri[:, :]).then_inc(sem("masks"), 1)
            e.tensor_copy(ident_b[:, :], ident[:, :]).then_inc(sem("masks"), 1)
            e.wait_ge(sem("masks"), 4)
            e.memset(tri[:, :], 1.0).then_inc(sem("blk"), 1)
            e.wait_ge(sem("blk"), 4)
            e.affine_select(out=tri[:, :], in_=tri[:, :], compare_op=ALU.is_ge, fill=0.0, base=0,
                            pattern=[[1, P]], channel_multiplier=-1).then_inc(sem("masks"), 1)
            c = [0]

            def step(ins):
                c[0] += 1
                ins.then_inc(sem("pool_step"), 1)
                e.wait_ge(sem("pool_step"), c[0])

            e.wait_ge(sem("s5_trig"), 2)
            e.wait_ge(sem("t_x"), 1)
            e.wait_ge(m_summed, MOD_WIDE)
            scr = [s5[:, 16 + k, :] for k in range(3)]
            er, ei = s5[:, 14, :], s5[:, 15, :]
            step(e.memset(ph_re[:, :, 0:1], 1.0))
            step(e.memset(ph_im[:, :, 0:1], 0.0))
            step(e.tensor_copy(er, s5[:, 3, :]))
            step(e.tensor_copy(ei, s5[:, 4, :]))
            ta = tiles(area(0, 4096))
            for m in range(8):
                n = 1 << m
                lo_r, lo_i = ph_re[:, :, 0:n], ph_im[:, :, 0:n]
                hi_r, hi_i = ph_re[:, :, n:2 * n], ph_im[:, :, n:2 * n]
                br, bi = bcast(er, n), bcast(ei, n)
                t1, t2 = ta[:, :, 0:n], ta[:, :, P:P + n]
                step(e.tensor_tensor(t1, lo_r, br, ALU.mult))
                step(e.tensor_tensor(t2, lo_i, bi, ALU.mult))
                step(e.tensor_tensor(hi_r, t1, t2, ALU.subtract))
                step(e.tensor_tensor(t1, lo_r, bi, ALU.mult))
                step(e.tensor_tensor(t2, lo_i, br, ALU.mult))
                step(e.tensor_tensor(hi_i, t1, t2, ALU.add))
                if m < 7:
                    step(e.tensor_tensor(scr[0], er, er, ALU.mult))
                    step(e.tensor_tensor(scr[1], ei, ei, ALU.mult))
                    step(e.tensor_tensor(scr[2], er, ei, ALU.mult))
                    step(e.tensor_tensor(er, scr[0], scr[1], ALU.subtract))
                    step(e.tensor_tensor(ei, scr[2], scr[2], ALU.add))
            e.wait_ge(sem("s5_quot"), 1)
            e.wait_ge(sem("ld_b"), 32)
            e.wait_ge(sem("b_zero"), 1)
            qr, qi = bcast(s5[:, 8, :], GCH), bcast(s5[:, 9, :], GCH)
            tb = area(0, 4 * ST * GCH).rearrange("p (q t c) -> p q t c", q=4, c=GCH)
            step(e.tensor_tensor(tb[:, 0], b_in[:, 0], qr, ALU.mult))
            step(e.tensor_tensor(tb[:, 1], b_in[:, 1], qi, ALU.mult))
            step(e.tensor_tensor(tb[:, 2], b_in[:, 0], qi, ALU.mult))
            step(e.tensor_tensor(tb[:, 3], b_in[:, 1], qr, ALU.mult))
            for g in range(2):
                rows, cols = slice(g * NST, (g + 1) * NST), slice(g * GCH, (g + 1) * GCH)
                step(e.tensor_tensor(b_bd[rows, 0, :, cols], tb[rows, 0], tb[rows, 1], ALU.subtract))
                ins = e.tensor_tensor(b_bd[rows, 1, :, cols], tb[rows, 2], tb[rows, 3], ALU.add)
                if g == 0:
                    step(ins)
                else:
                    ins.then_inc(sem("b_bd_ok"), 1)
            e.wait_ge(sem("b_bd_ok"), 1)
            e.wait_ge(gu_free, GU_BASE["w_in"] + 8)
            z = proj[:, 4:8, :]
            w = [bcast(vec(v1, V1, "conv_w", 4 * k, 4), S) for k in range(3)]
            t1 = proj[:, 8:12, :]
            acc = conv_sum[:, :, :]
            cs = sem("conv_ok")
            e.tensor_tensor(z, z, t1, ALU.mult).then_inc(cs, 1)
            e.wait_ge(cs, 1)
            e.tensor_tensor(acc, z, w[2], ALU.mult).then_inc(cs, 1)
            e.tensor_tensor(t1, z, w[1], ALU.mult).then_inc(cs, 1)
            e.wait_ge(cs, 3)
            e.tensor_tensor(acc[:, :, 1:S], acc[:, :, 1:S], t1[:, :, 0:S - 1], ALU.add).then_inc(cs, 1)
            e.wait_ge(cs, 4)
            e.tensor_tensor(t1, z, w[0], ALU.mult).then_inc(cs, 1)
            e.wait_ge(cs, 5)
            e.tensor_tensor(acc[:, :, 2:S], acc[:, :, 2:S], t1[:, :, 0:S - 2], ALU.add).then_inc(cs, 1)
            e.wait_ge(cs, 6)
            e.tensor_tensor(proj[:, 0:4, :], proj[:, 0:4, :], acc, ALU.mult).then_inc(cs, 1)



_INS = [
    "x", "cond", "w_mod", "b_mod", "ffn1_norm", "ffn1_w_gate", "ffn1_w_up", "ffn1_w_down", "mix_norm", "w_in",
    "conv_w", "lambda_re", "lambda_im", "log_dt", "ssm_b_re", "ssm_b_im", "ssm_c_re", "ssm_c_im", "ssm_d", "glu_w",
    "glu_b", "out_norm_conv", "out_norm_ssm", "w_out", "ffn2_norm", "ffn2_w_gate", "ffn2_w_up", "ffn2_w_down",
    "final_norm", "a_norm_2", "a_w_in_2", "a_w_gate_up_2", "a_b_gate_2", "a_head_norm_2", "a_w_out_2",
    "kv_norm_2", "w_kv_2", "k_norm_2", "b_norm_2", "b_w_q_2", "b_q_norm_2", "b_lambda_2", "b_head_norm_2",
    "b_w_out_2", "mlp_norm_2", "mlp_w1_2", "mlp_w2_2",
]


def kernel(**inputs):
    import concourse.bacc as bacc
    import numpy as np
    from concourse.bass_utils import run_bass_kernel_spmd

    nc = bacc.Bacc("TRN2", target_bir_lowering=False, num_devices=1)
    arrays, tensors = {}, {}
    for name in _INS:
        a = np.ascontiguousarray(inputs[name])
        arrays[f"in_{name}"] = a
        tensors[name] = nc.dram_tensor(f"in_{name}", a.shape, mybir.dt.from_np(a.dtype), kind="ExternalInput").ap()
    out = nc.dram_tensor("out_0", (1, S, D), F32, kind="ExternalOutput").ap()
    build(nc, tensors, out)
    r = run_bass_kernel_spmd(nc, [arrays], core_ids=[0])
    return r.results[0]["out_0"]
```
